# Optimizing a Trainium2 kernel written in Bass

```python
import math
import jax, jax.numpy as jnp
from jax import lax
import numpy as np

D_MODEL = 1024
BATCH = 1
SEQ = 256
DEPTH = 1

N_HEADS = 8
HEAD_DIM = 64
ATTN_WIDTH = N_HEADS * HEAD_DIM
MOBA_BLOCK = 256
MOBA_TOPK = 3
Q_CHUNK = 64
NUM_BUCKETS = 32
MAX_DISTANCE = 128
POOL_WINDOWS = (2, 4, 8, 16)
POOL_GROUPS = 4
POOL_GROUP_DIM = 128
POOL_WIDTH = POOL_GROUPS * POOL_GROUP_DIM
N_BRANCHES = 2
IN_COLS = 3 * ATTN_WIDTH + POOL_WIDTH + N_BRANCHES * D_MODEL
N_EXPERTS = 32
TOP_K = 4
D_EXPERT = D_MODEL
SWIGLU_LIMIT = 7.0
SWIGLU_ALPHA = 1.702
EXPERT_BLOCK = 128
PLE_DIM = 256
RMS_EPS = 1e-6

kernel_name = "hybrid_moba_pool_moe_block"

def rms_norm(x, g):
    xf = x.astype(jnp.float32)
    y = xf * lax.rsqrt(jnp.mean(xf * xf, axis=-1, keepdims=True) + RMS_EPS)
    return (y * g.astype(jnp.float32)).astype(x.dtype)

def t5_causal_bucket(rel):
    n = jnp.maximum(rel, 0)
    max_exact = NUM_BUCKETS // 2
    nf = jnp.maximum(n, 1).astype(jnp.float32)
    large = max_exact + (jnp.log(nf / max_exact) / math.log(MAX_DISTANCE / max_exact)
                         * (NUM_BUCKETS - max_exact)).astype(jnp.int32)
    large = jnp.minimum(large, NUM_BUCKETS - 1)
    return jnp.where(n < max_exact, n, large)

def moba_attention(q, k, v, rel_bias):
    b, h, s, dh = q.shape
    nb = -(-s // MOBA_BLOCK)
    s_pad = nb * MOBA_BLOCK
    k_eff = min(MOBA_TOPK, nb)
    pad = ((0, 0), (0, 0), (0, s_pad - s), (0, 0))
    k = jnp.pad(k, pad)
    v = jnp.pad(v, pad)
    k_blocks = k.reshape(b, h, nb, MOBA_BLOCK, dh)
    v_blocks = v.reshape(b, h, nb, MOBA_BLOCK, dh)
    k_mean = jnp.mean(k_blocks.astype(jnp.float32), axis=3)
    bias_t = rel_bias.astype(jnp.float32).T
    b_idx = jnp.arange(b)[:, None, None, None]
    h_idx = jnp.arange(h)[None, :, None, None]
    scale = dh ** -0.5
    neg = jnp.finfo(jnp.float32).min
    in_block = jnp.arange(MOBA_BLOCK)
    n_sel = k_eff * MOBA_BLOCK

    def chunk(c):
        q0 = c * Q_CHUNK
        j = q0 // MOBA_BLOCK
        qc = lax.dynamic_slice_in_dim(q, q0, Q_CHUNK, axis=2).astype(jnp.float32) * scale
        qpos = q0 + jnp.arange(Q_CHUNK)
        gate = jnp.einsum('bhqd,bhnd->bhqn', qc, k_mean)
        gate = jnp.where(jnp.arange(nb) < j, gate, neg)
        _, sel = lax.top_k(gate, k_eff)
        valid = jnp.arange(k_eff) < j
        k_sel = k_blocks[b_idx, h_idx, sel].astype(jnp.float32)
        v_sel = v_blocks[b_idx, h_idx, sel].astype(jnp.float32)
        s_sel = jnp.einsum('bhqd,bhqnkd->bhqnk', qc, k_sel)
        rel_sel = qpos[:, None, None] - (sel[..., None] * MOBA_BLOCK + in_block)
        s_sel = s_sel + bias_t[h_idx[..., None], t5_causal_bucket(rel_sel)]
        s_sel = jnp.where(valid[:, None], s_sel, neg)
        k_own = lax.dynamic_slice_in_dim(k, j * MOBA_BLOCK, MOBA_BLOCK, axis=2).astype(jnp.float32)
        v_own = lax.dynamic_slice_in_dim(v, j * MOBA_BLOCK, MOBA_BLOCK, axis=2).astype(jnp.float32)
        rel_own = qpos[:, None] - (j * MOBA_BLOCK + in_block)[None, :]
        s_own = jnp.einsum('bhqd,bhkd->bhqk', qc, k_own) + bias_t[:, t5_causal_bucket(rel_own)]
        s_own = jnp.where(rel_own >= 0, s_own, neg)
        logits = jnp.concatenate([s_sel.reshape(b, h, Q_CHUNK, n_sel), s_own], axis=-1)
        probs = jax.nn.softmax(logits, axis=-1)
        p_sel = probs[..., :n_sel].reshape(b, h, Q_CHUNK, k_eff, MOBA_BLOCK)
        p_own = probs[..., n_sel:]
        return (jnp.einsum('bhqnk,bhqnkd->bhqd', p_sel, v_sel)
                + jnp.einsum('bhqk,bhkd->bhqd', p_own, v_own))

    out = lax.map(chunk, jnp.arange(s // Q_CHUNK))
    out = out.transpose(1, 0, 3, 2, 4).reshape(b, s, h * dh)
    return out.astype(q.dtype)

def causal_multiscale_pool(u):
    b, s, _ = u.shape
    ug = u.astype(jnp.float32).reshape(b, s, POOL_GROUPS, POOL_GROUP_DIM)
    csum = jnp.concatenate([jnp.zeros((b, 1, POOL_GROUPS, POOL_GROUP_DIM), jnp.float32),
                            jnp.cumsum(ug, axis=1)], axis=1)
    t = jnp.arange(s)
    w = jnp.array(POOL_WINDOWS, dtype=jnp.int32)
    lo = jnp.maximum(t[:, None] + 1 - w[None, :], 0)
    cnt = jnp.minimum(t[:, None] + 1, w[None, :]).astype(jnp.float32)
    g_idx = jnp.arange(POOL_GROUPS)[None, :]
    window_sum = csum[:, 1:] - csum[:, lo, g_idx]
    return window_sum / cnt[None, :, :, None] - ug

def moe_ffn(hf, router_w, router_b, w_gate_up, b_gate_up, w_down, b_down):
    t, d = hf.shape
    logits = (hf @ router_w + router_b).astype(jnp.float32)
    top_vals, top_idx = lax.top_k(logits, TOP_K)
    gates = jax.nn.softmax(top_vals, axis=-1).astype(hf.dtype)
    n_assign = t * TOP_K
    flat_e = top_idx.reshape(-1)
    flat_tok = jnp.arange(n_assign, dtype=jnp.int32) // TOP_K
    flat_w = gates.reshape(-1)
    order = jnp.argsort(flat_e)
    sorted_e = flat_e[order]
    counts = jnp.bincount(flat_e, length=N_EXPERTS)
    starts = jnp.cumsum(counts) - counts
    padded = (counts + EXPERT_BLOCK - 1) // EXPERT_BLOCK * EXPERT_BLOCK
    pend = jnp.cumsum(padded)
    pstart = pend - padded
    dest = pstart[sorted_e] + jnp.arange(n_assign) - starts[sorted_e]
    n_pad = n_assign + N_EXPERTS * EXPERT_BLOCK
    n_blk = n_pad // EXPERT_BLOCK
    row_tok = jnp.zeros((n_pad,), jnp.int32).at[dest].set(flat_tok[order])
    row_w = jnp.zeros((n_pad,), hf.dtype).at[dest].set(flat_w[order])
    blk_expert = jnp.minimum(
        jnp.searchsorted(pend, jnp.arange(n_blk) * EXPERT_BLOCK, side='right'), N_EXPERTS - 1)

    def run_block(args):
        tok, wt, e = args
        xb = hf[tok]
        gu = xb @ w_gate_up[e] + b_gate_up[e]
        glu_in = jnp.minimum(gu[:, 0::2], SWIGLU_LIMIT)
        lin = jnp.clip(gu[:, 1::2], -SWIGLU_LIMIT, SWIGLU_LIMIT)
        hid = (lin + 1) * (glu_in * jax.nn.sigmoid(SWIGLU_ALPHA * glu_in))
        y = hid @ w_down[e] + b_down[e]
        return y * wt[:, None]

    ys = lax.map(run_block, (row_tok.reshape(n_blk, EXPERT_BLOCK),
                             row_w.reshape(n_blk, EXPERT_BLOCK), blk_expert))
    return jax.ops.segment_sum(ys.reshape(n_pad, d), row_tok, num_segments=t)

def setup_inputs(seed: int = 0) -> dict:
    key = jax.random.key(seed)
    ks = jax.random.split(key, 24)

    def nrm(k, shape, scale):
        return jax.random.normal(k, shape, jnp.float32) * scale

    D, E, F = D_MODEL, N_EXPERTS, D_EXPERT
    return {
        "x": nrm(ks[0], (BATCH, SEQ, D), 1.0),
        "p": nrm(ks[1], (DEPTH, BATCH, SEQ, PLE_DIM), 1.0),
        "rel_bias": nrm(ks[2], (NUM_BUCKETS, N_HEADS), 0.5),
        "norm_mix_g": 1.0 + nrm(ks[3], (DEPTH, D), 0.05),
        "w_in": nrm(ks[4], (DEPTH, D, IN_COLS), D ** -0.5),
        "pool_w": nrm(ks[5], (DEPTH, POOL_GROUPS, POOL_GROUP_DIM, POOL_GROUP_DIM), POOL_GROUP_DIM ** -0.5),
        "pool_scale": 1.0 + nrm(ks[6], (DEPTH, POOL_WIDTH), 0.1),
        "w_o_attn": nrm(ks[7], (DEPTH, ATTN_WIDTH, D), ATTN_WIDTH ** -0.5),
        "w_o_pool": nrm(ks[8], (DEPTH, POOL_WIDTH, D), POOL_WIDTH ** -0.5),
        "w_out": nrm(ks[9], (DEPTH, D, D), D ** -0.5),
        "norm_ffn_g": 1.0 + nrm(ks[10], (DEPTH, D), 0.05),
        "router_w": nrm(ks[11], (DEPTH, D, E), D ** -0.5),
        "router_b": nrm(ks[12], (DEPTH, E), 0.01),
        "w_gate_up": nrm(ks[13], (DEPTH, E, D, 2 * F), D ** -0.5),
        "b_gate_up": nrm(ks[14], (DEPTH, E, 2 * F), 0.02),
        "w_down": nrm(ks[15], (DEPTH, E, F, D), F ** -0.5),
        "b_down": nrm(ks[16], (DEPTH, E, D), 0.02),
        "norm_ple_g": 1.0 + nrm(ks[17], (DEPTH, D), 0.05),
        "w_ple_gate": nrm(ks[18], (DEPTH, D, D), D ** -0.5),
        "w_ple_proj": nrm(ks[19], (DEPTH, PLE_DIM, D), PLE_DIM ** -0.5),
        "norm_final_g": 1.0 + nrm(ks[20], (D,), 0.05),
    }

def reference(x, p, rel_bias, norm_mix_g, w_in, pool_w, pool_scale, w_o_attn, w_o_pool, w_out,
              norm_ffn_g, router_w, router_b, w_gate_up, b_gate_up, w_down, b_down,
              norm_ple_g, w_ple_gate, w_ple_proj, norm_final_g):
    b, s, d = x.shape
    cuts = [ATTN_WIDTH, 2 * ATTN_WIDTH, 3 * ATTN_WIDTH, 3 * ATTN_WIDTH + POOL_WIDTH]

    def heads(t):
        return t.reshape(b, s, N_HEADS, HEAD_DIM).transpose(0, 2, 1, 3)

    for i in range(DEPTH):
        h = rms_norm(x, norm_mix_g[i])
        q, k, v, u, g = jnp.split(h @ w_in[i], cuts, axis=-1)
        attn = moba_attention(heads(q), heads(k), heads(v), rel_bias)
        pooled = jnp.einsum('bsgc,gcd->bsgd', causal_multiscale_pool(u),
                            pool_w[i].astype(jnp.float32)).reshape(b, s, POOL_WIDTH)
        pooled = (pooled * pool_scale[i].astype(jnp.float32)).astype(x.dtype)
        gates = jax.nn.sigmoid(g.reshape(b, s, N_BRANCHES, d))
        merged = gates[:, :, 0] * (attn @ w_o_attn[i]) + gates[:, :, 1] * (pooled @ w_o_pool[i])
        x = x + merged @ w_out[i]
        hf = rms_norm(x, norm_ffn_g[i]).reshape(b * s, d)
        x = x + moe_ffn(hf, router_w[i], router_b[i], w_gate_up[i], b_gate_up[i],
                        w_down[i], b_down[i]).reshape(b, s, d)
        hp = rms_norm(x, norm_ple_g[i])
        x = x + jax.nn.sigmoid(hp @ w_ple_gate[i]) * (p[i] @ w_ple_proj[i])
    return rms_norm(x, norm_final_g)


_drawn_inputs = setup_inputs


def setup_inputs(seed=0):
    import zlib

    import numpy as np

    out = dict(_drawn_inputs(seed))
    spreads = {}
    factors = {'router_b': 2.729, 'b_gate_up': 6.04, 'b_down': 6.945, 'norm_ple_g': 7.255}
    for name, (base, spread) in spreads.items():
        noise = np.random.default_rng([zlib.crc32(name.encode()), seed]).standard_normal(out[name].shape)
        drawn = base * np.exp(spread * noise) if base else spread * noise
        out[name] = __import__('jax').numpy.asarray(drawn.astype(out[name].dtype))
    for name, factor in factors.items():
        out[name] = (out[name] * factor).astype(out[name].dtype)
    return out
```

```python
import math
from contextlib import ExitStack

import numpy as np

import concourse.bass as bass
from concourse import mybir

P = 128
D = 1024
T = 256
TB = T // P
KD = D // P
HEADS = 8
DH = 64
AW = HEADS * DH
NW = 2 * D
BUCKETS = 32
MAX_DISTANCE = 128
WINDOWS = (2, 4, 8, 16)
GROUPS = len(WINDOWS)
E = 32
TOP_K = 4
SLOTS = 64
N_EXTRA = 16
LIMIT = 7.0
ALPHA = 1.702
PLE = 256
EPS = 1e-6
NEG = -3.0e38
BANK = 512

C_MIX, C_FFN, C_PLE, C_POOL, C_RW, C_BGU = 0, 8, 16, 24, 28, 28 + KD * E
N_PACK = C_BGU + E * 16

ALU = mybir.AluOpType
ACT = mybir.ActivationFunctionType
AX = mybir.AxisListType.X
F32 = mybir.dt.float32
I32 = mybir.dt.int32
U32 = mybir.dt.uint32


class Chain:

    def __init__(self, eng, sem):
        self.eng, self.sem, self.n = eng, sem, 0

    def __call__(self, ins):
        ins.then_inc(self.sem, 1)
        self.n = self.n + 1
        self.eng.wait_ge(self.sem, self.n)


def wait_pos(eng, sem, value):
    if not isinstance(value, int) or value > 0:
        eng.wait_ge(sem, value)


def block_kernel(nc, x, x_t, p_t, pack, rel_bias, bucket_of, w_in, pool_w, w_o_attn, w_o_pool, w_out,
                 router_b, w_gate_up, w_down, b_down, w_ple_gate, w_ple_proj, norm_final_g, out):
    ctx = ExitStack()
    with ctx:
        def sb(name, shape, dt=F32):
            return ctx.enter_context(nc.sbuf_tensor(name, shape, dt))

        def sem(name):
            return ctx.enter_context(nc.semaphore(name))

        bias_rows = nc.dram_tensor("bias_rows", (HEADS, P, 384), F32).ap()

        ring = sb("ring", [P, 20, NW])
        acc = sb("acc", [P, TB, D])
        hfn = sb("hfn", [P, TB, D])
        mid = sb("mid", [P, 2048])
        consts = sb("consts", [P, N_PACK])
        xg = sb("xg", [P, 2, KD, SLOTS])
        gu_sb = sb("gu_sb", [P, 2 * BANK])
        y_sb = sb("y_sb", [P, BANK])
        sel = sb("sel", [P, T])
        pick = sb("pick", [P, 2, TB, SLOTS])
        pick_g = sb("pick_g", [P, TB, 2, SLOTS])
        hot = sb("hot", [P, TB * TOP_K, E])
        hot_g = sb("hot_g", [P, TB * TOP_K, E])
        chosen = sb("chosen", [P, TB, E])
        gates = sb("gates", [P, TB, E])
        rank1 = sb("rank1", [P, TB, E])
        small = sb("small", [P, 96])
        iota1 = sb("iota1", [P, T])
        ident = sb("ident", [P, P])
        tri = sb("tri", [P, P])
        ones = sb("ones", [P, P])
        relb = sb("relb", [BUCKETS, HEADS])
        row256 = sb("row256", [P, T])
        rb_bc = sb("rb_bc", [P, E])
        lists = sb("lists", [1, 2 * N_EXTRA + 1], I32)

        h_t = ring[:, 12, :].rearrange("p (c t) -> p c t", c=KD)
        q_t = ring[:, 13, 0:1024].rearrange("p (c t) -> p c t", c=4)
        k_t = ring[:, 13, 1024:2048].rearrange("p (c t) -> p c t", c=4)
        v_n = ring[:, 14, 0:1024].rearrange("p (b n) -> p b n", b=TB)
        u_t = ring[:, 14, 1024:2048].rearrange("p (g t) -> p g t", g=GROUPS)
        g_t = ring[:, 15:17, :].rearrange("p s n -> p (s n)").rearrange("p (c t) -> p c t", t=T)
        bias = ring[:, 17, :].rearrange("p (h k) -> p h k", h=HEADS)
        pool2_t = ring[:, 17, 0:1024].rearrange("p (g t) -> p g t", g=GROUPS)
        prob1 = ring[:, 18, :].rearrange("p (h k) -> p h k", h=HEADS)
        prob0 = ring[:, 19, 0:1024].rearrange("p (h k) -> p h k", h=HEADS)
        attn_t = ring[:, 19, 1024:2048].rearrange("p (c t) -> p c t", c=4)
        prob_t = ring[:, 12:14, :].rearrange("p s n -> p (s n)")[:, 0:24 * P].rearrange("p (j q) -> p j q", q=P)
        x_raw = ring[:, 18, :].rearrange("p (c t) -> p c t", c=KD)
        x_sq = ring[:, 16, :].rearrange("p (c t) -> p c t", c=KD)
        win_a = hfn[:, 0, :].rearrange("p (g t) -> p g t", g=GROUPS)
        win_b = hfn[:, 1, :].rearrange("p (g t) -> p g t", g=GROUPS)
        inv_cnt = gu_sb[:, :].rearrange("p (g t) -> p g t", g=GROUPS)
        pooled = xg[:, :, :, :].rearrange("p a c s -> p (a c s)").rearrange("p (g t) -> p g t", g=GROUPS)
        branch = xg[:, 0, :, :].rearrange("p c s -> p (c s)")
        pw_sb = y_sb[:, :].rearrange("p (g d) -> p g d", g=GROUPS)
        onehot = hot[0:BUCKETS, :, :].rearrange("p a e -> p (a e)")
        bias_v = xg[0:HEADS, :, :, :].rearrange("p a c s -> p (a c s)")[:, 0:384]
        merged = mid[:, :].rearrange("p (c t) -> p c t", c=KD)
        hf_t = merged
        gate_rows = row256[0:E, :]
        g_act, l_act, sg, hid = (mid[:, i * BANK:(i + 1) * BANK] for i in range(4))
        bd_half = (y_sb[0:E, :], hid[0:E, :])
        wpg = ring[:, 8:12, :].rearrange("p s (j n) -> p (s j) n", j=2)
        wpp = ring[:, 12, :].rearrange("p (j n) -> p j n", j=2)
        pt_sb = ring[:, 13, 0:512].rearrange("p (j t) -> p j t", j=2)
        fg_bc = ring[:, 13, 1024:2048]
        pproj = ring[:, 14, :].rearrange("p (b n) -> p b n", b=TB)
        gate_s = ring[:, 15, :].rearrange("p (b n) -> p b n", b=TB)
        hp_t = mid[:, :].rearrange("p (c b t) -> p c b t", c=KD, b=TB)

        def stat(a, n=1):
            return small[:, a:a + n]

        ps = ctx.enter_context(nc.psum_tensor("ps", [P, 8 * BANK], F32))

        def bank(b, n=1):
            return ps[:, b * BANK:(b + n) * BANK]

        s_xt, s_pack, s_pw, s_x, s_relb, s_rb, s_bd = (sem(n) for n in (
            "xt_landed", "pack_landed", "pool_w_landed", "x_landed", "rel_landed", "router_b_landed",
            "b_down_landed"))
        s_bias_out, s_bias_in = sem("bias_rows_stored"), sem("bias_landed")
        s_qkvu = [sem(f"qkvu_landed{k}") for k in range(KD)]
        s_g = [sem(f"g_landed{k}") for k in range(KD)]
        s_wo = [sem(f"wo_landed{i}") for i in range(4)]
        s_wout = [sem(f"wout_landed{i}") for i in range(4)]
        s_gu = [[sem(f"gu_landed{h}_{k}") for k in range(KD)] for h in range(2)]
        s_dn = [sem(f"down_landed{u}") for u in range(4)]
        s_ple = [sem(f"ple_landed{i}") for i in range(4)]
        s_ple_small = [sem(f"ple_small_landed{i}") for i in range(3)]
        s_out = sem("out_stored")

        consts_made, eps_ready = sem("consts_made"), sem("eps_ready")
        dve_chain, dve_tail_chain, pool_chain = sem("dve_chain"), sem("dve_tail_chain"), sem("pool_chain")
        squared = sem("squared")
        sumsq_done = sem("sumsq_done")
        rms_sqrt = sem("rms_sqrt")
        h_ready = sem("h_ready")
        bias_mm, bias_copied = sem("bias_mm"), sem("bias_copied")
        qkvu_used, qkvu_out = sem("qkvu_used"), sem("qkvu_evacuated")
        u_out = sem("u_evacuated")
        g_done, g_out = sem("g_done"), sem("g_evacuated")
        cnt_ready, inv_ready, pooled_ready = sem("cnt_ready"), sem("inv_ready"), sem("pooled_ready")
        scores_done, max_ready, exp_done, prob_ready = (sem(n) for n in (
            "scores_done", "max_ready", "exp_done", "prob_ready"))
        probt_done, probt_out = sem("prob_t_done"), sem("prob_t_evacuated")
        pv_done, attn_out = sem("pv_done"), sem("attn_evacuated")
        ao_done, po_done, merged_ready = sem("attn_branch_done"), sem("pool_branch_done"), sem("merged_ready")
        wout_done, x1_ready = sem("wout_done"), sem("x1_ready")
        sq_ready, var_ready, sqrt_ready, norm_ready = (sem(n) for n in (
            "sumsq_ready", "var_ready", "sqrt_ready", "norm_ready"))
        turned, turned_out = sem("norm_turned"), sem("norm_turned_evacuated")
        logits_done, top_ready, gexp_ready, chosen_ready, gates_ready = (sem(n) for n in (
            "logits_done", "top_ready", "gate_exp_ready", "chosen_ready", "gates_ready"))
        rank_done, rank_ready, count_done, gates_turned, gate_rows_ready = (sem(n) for n in (
            "rank_done", "rank_ready", "count_done", "gates_turned", "gate_rows_ready"))
        counts_read, lists_ready = sem("counts_read"), sem("lists_ready")
        pick_ready, gath_done, xg_ready = sem("pick_ready"), sem("gather_done"), sem("xg_ready")
        pickg_ready, selt_done, sel_ready = sem("pick_g_ready"), sem("sel_turned"), sem("sel_ready")
        gu_used, gu_out, gut_done, gut_read = (sem(n) for n in (
            "gu_used", "gu_evacuated", "gu_turned", "gu_turned_read"))
        glu_ready, sig_ready, hid_ready = sem("glu_ready"), sem("sigmoid_ready"), sem("hid_ready")
        dn_used, y_ready, scat_done, added = (sem(n) for n in ("down_used", "y_ready", "scatter_done", "added"))
        pproj_done, pproj_out = sem("ple_proj_done"), sem("ple_proj_evacuated")
        gate_done, gate_out, x3_ready, fin_ready = (sem(n) for n in (
            "ple_gate_done", "ple_gate_sigmoid", "x3_ready", "final_ready"))

        block = ctx.enter_context(nc.Block())

        wo_units = [(w_o_attn, 0), (w_o_attn, 1), (w_o_pool, 0), (w_o_pool, 1)]

        def two_chunks(w, u):
            return w[2 * u * P:(2 * u + 2) * P, :].rearrange("(j p) n -> p j n", p=P)

        def slot2(s):
            return ring[:, s, :].rearrange("p (j n) -> p j n", j=2)

        @block.sync
        def _(sp):
            def load_gu(e, h, k, landed):
                src = w_gate_up[e] if isinstance(e, int) else w_gate_up[bass.ds(e, 1)].rearrange("o d f -> (o d) f")
                sp.dma_start(ring[:, 8 * h + k, :], src[k * P:(k + 1) * P, :]).then_inc(landed, 16)

            def load_down(e, u, landed):
                src = w_down[e] if isinstance(e, int) else w_down[bass.ds(e, 1)].rearrange("o d f -> (o d) f")
                sp.dma_start(slot2(16 + u), two_chunks(src, u)).then_inc(landed, 16)

            sp.dma_start(x_raw, x_t.rearrange("(c p) t -> p c t", p=P)).then_inc(s_xt, 16)
            sp.dma_start(consts[:, :], pack).then_inc(s_pack, 16)
            for k in range(KD):
                sp.dma_start(ring[:, k, :], w_in[k * P:(k + 1) * P, 0:NW]).then_inc(s_qkvu[k], 16)
            sp.dma_start(pw_sb, pool_w.rearrange("g c d -> c g d")).then_inc(s_pw, 16)
            sp.dma_start(acc[:, :, :], x.rearrange("(b p) d -> p b d", p=P)).then_inc(s_x, 16)
            sp.dma_start(rb_bc[:, :], router_b.partition_broadcast(P)).then_inc(s_rb, 16)
            for k in range(KD):
                if k >= 4:
                    sp.wait_ge(qkvu_used, k - 3)
                sp.dma_start(ring[:, (8 + k) % 12, :], w_in[k * P:(k + 1) * P, NW:2 * NW]).then_inc(s_g[k], 16)
            for i, (w, u) in enumerate(wo_units):
                sp.wait_ge(qkvu_used, 5 + i)
                sp.dma_start(slot2(4 + i), two_chunks(w, u)).then_inc(s_wo[i], 16)
            sp.wait_ge(g_done, 8)
            for i in range(4):
                sp.dma_start(slot2(8 + i), two_chunks(w_out, i)).then_inc(s_wout[i], 16)
            for k in range(4):
                load_gu(0, 0, k, s_gu[0][k])
            for k in range(4, KD):
                sp.wait_ge(ao_done if k < 6 else po_done, 4)
                load_gu(0, 0, k, s_gu[0][k])
            sp.wait_ge(merged_ready, 4)
            for u in range(4):
                load_down(0, u, s_dn[u])
            for k in range(4, KD):
                load_gu(1, 1, k, s_gu[1][k])
            sp.wait_ge(wout_done, 2)
            for k in range(4):
                load_gu(1, 1, k, s_gu[1][k])

            sp.wait_ge(g_done, 10)
            sp.wait_ge(logits_done, 1)
            for half in range(2):
                sp.dma_start(bd_half[half], b_down[:, half * BANK:(half + 1) * BANK]).then_inc(s_bd, 16)

            def loads(e, h):
                for k in range(KD):
                    sp.wait_ge(gu_used, (e - 2) * KD + k + 1)
                    load_gu(e, h, k, s_gu[h][k])
                for u in range(4):
                    sp.wait_ge(dn_used, (e - 2) * 4 + u + 1)
                    load_down(e - 1, u, s_dn[u])

            with sp.Fori(1, E // 2) as it:
                for h in range(2):
                    loads(2 * it + h, h)
            for u in range(4):
                sp.wait_ge(dn_used, (E - 2) * 4 + u + 1)
                load_down(E - 1, u, s_dn[u])
            sp.wait_ge(gu_used, E * KD)
            sp.dma_start(pt_sb, p_t.rearrange("(j p) t -> p j t", p=P)).then_inc(s_ple_small[0], 16)
            sp.dma_start(wpp, w_ple_proj.rearrange("(j p) n -> p j n", p=P)).then_inc(s_ple_small[1], 16)
            for i in range(4):
                sp.dma_start(slot2(8 + i), two_chunks(w_ple_gate, i)).then_inc(s_ple[i], 16)
            sp.dma_start(fg_bc, norm_final_g.partition_broadcast(P)).then_inc(s_ple_small[2], 16)

            sp.wait_ge(lists_ready, 1)
            n_extra = sp.value_load(lists[0:1, 2 * N_EXTRA:2 * N_EXTRA + 1], min_val=0, max_val=N_EXTRA)
            with sp.If(n_extra > 0):
                with sp.Fori(0, n_extra) as i:
                    e = sp.value_load(lists[0:1, bass.ds(i, 1)], min_val=0, max_val=E - 1)
                    sp.wait_ge(gu_used, (i + E) * KD)
                    for k in range(KD):
                        load_gu(e, 0, k, s_gu[0][k])
                    sp.wait_ge(dn_used, (i + E) * 4)
                    for u in range(4):
                        load_down(e, u, s_dn[u])

            for b in range(TB):
                sp.wait_ge(fin_ready, b + 1)
                sp.dma_start(out[b * P:(b + 1) * P, :], acc[:, b, :]).then_inc(s_out, 16)
            sp.wait_ge(s_out, 32)

        @block.gpsimd
        def _(pool):
            chain = Chain(pool, pool_chain)
            pool.memset(ones[:, :], 1.0).then_inc(consts_made, 1)
            chain(pool.memset(ident[:, :], 0.0))
            chain(pool.affine_select(out=ident[:, :], in_=ident[:, :], compare_op=ALU.not_equal, fill=1.0,
                                     base=0, pattern=[[-1, P]], channel_multiplier=1))
            pool.wait_ge(consts_made, 1)
            chain(pool.affine_select(out=tri[:, :], in_=ones[:, :], compare_op=ALU.is_gt, fill=0.0,
                                     base=0, pattern=[[1, P]], channel_multiplier=-1))
            chain(pool.iota(iota1[:, :], pattern=[[1, T]], base=1, channel_multiplier=0,
                            allow_small_or_imprecise_dtypes=True))
            pool.memset(bias_v[:, 256:384], NEG).then_inc(consts_made, 1)
            for g, w in enumerate(WINDOWS):
                last = pool.tensor_scalar(inv_cnt[:, g, :], iota1[:, :], float(w), None, ALU.min)
            last.then_inc(cnt_ready, 1)

            pool.wait_ge(u_out, 2)
            src = u_t
            for j in range(GROUPS):
                dst = (win_a, win_b)[j % 2]
                sh = 1 << j
                pool.tensor_copy(dst[:, j:, 0:sh], src[:, j:, 0:sh])
                chain(pool.tensor_tensor(dst[:, j:, sh:], src[:, j:, sh:], src[:, j:, 0:T - sh], ALU.add))
                if j == 0:
                    pool.wait_ge(inv_ready, 1)
                chain(pool.tensor_tensor(pooled[:, j, :], dst[:, j, :], inv_cnt[:, j, :], ALU.mult))
                last = pool.tensor_tensor(pooled[:, j, :], pooled[:, j, :], u_t[:, j, :], ALU.subtract)
                src = dst
            last.then_inc(pooled_ready, 1)

        @block.scalar
        def _(act):
            act.dma_start(relb[:, :], rel_bias).then_inc(s_relb, 16)
            act.dma_start(onehot, bucket_of).then_inc(s_relb, 16)
            act.wait_ge(s_xt, 16)
            for c in range(0, KD, 2):
                act.activation(x_sq[:, c, :], x_raw[:, c, :], ACT.Square).then_inc(squared, 1)
            act.wait_ge(sumsq_done, 1)
            act.wait_ge(eps_ready, 1)
            act.activation(row256[:, :], bank(0)[:, 0:T], ACT.Sqrt, bias=stat(0), scale=1.0 / D).then_inc(rms_sqrt, 1)
            act.wait_ge(bias_mm, 1)
            act.wait_ge(consts_made, 2)
            act.activation(bias_v[:, 0:256], bank(1)[0:HEADS, 0:256], ACT.Copy).then_inc(bias_copied, 1)
            act.wait_ge(bias_copied, 1)
            act.dma_start(bias_rows[:, :, :], bias_v.unsqueeze(1).to_broadcast([HEADS, P, 384])).then_inc(s_bias_out, 16)
            act.wait_ge(s_bias_out, 16)
            for par in range(2):
                src = bass.AP(tensor=bias_rows.tensor, offset=par * P * 384 + P - 1,
                              ap=[[384 - 1, P], [2 * P * 384, 4], [1, T]])
                act.dma_start(bias[:, 4 * par:4 * par + 4, :], src).then_inc(s_bias_in, 16)
            act.wait_ge(qkvu_used, KD)
            act.activation(u_t[:, 0:2, :].rearrange("p c t -> p (c t)"), bank(6), ACT.Copy).then_inc(u_out, 1)
            act.activation(q_t[:, 0:2, :].rearrange("p c t -> p (c t)"), bank(0), ACT.Copy).then_inc(qkvu_out, 1)
            act.activation(k_t[:, 0:2, :].rearrange("p c t -> p (c t)"), bank(2), ACT.Copy).then_inc(qkvu_out, 1)
            act.activation(v_n[:, 0, :], bank(4), ACT.Copy).then_inc(qkvu_out, 1)

            def g_sigmoid(i):
                act.wait_ge(g_done, i + 1)
                act.activation(g_t[:, 2 * i:2 * i + 2, :].rearrange("p c t -> p (c t)"), bank(6 + i % 2),
                               ACT.Sigmoid).then_inc(g_out, 1)

            g_sigmoid(0)
            g_sigmoid(1)
            act.wait_ge(max_ready, 1)
            for h in range(HEADS):
                act.activation(prob1[:, h, :], prob1[:, h, :], ACT.Exp, bias=stat(40 + h),
                               accum_out=stat(56 + h)).then_inc(exp_done, 1)
            act.wait_ge(max_ready, 2)
            for h in range(HEADS):
                act.activation(prob0[:, h, :], prob0[:, h, :], ACT.Exp, bias=stat(48 + h),
                               accum_out=stat(64 + h)).then_inc(exp_done, 1)
            for i in range(2, 8):
                g_sigmoid(i)
            for i in (8, 9):
                act.wait_ge(g_done, i + 1)
                for j in range(2):
                    g = 2 * (i - 8) + j
                    last = act.activation(pool2_t[:, g, :], bank(6 + i % 2)[:, j * T:(j + 1) * T], ACT.Copy,
                                          scale=consts[:, C_POOL + g:C_POOL + g + 1])
                last.then_inc(g_out, 1)
            for i in range(0, 6, 2):
                act.wait_ge(probt_done, i + 1)
                act.activation(prob_t[:, 4 * i:4 * i + 4, :].rearrange("p j q -> p (j q)"), bank(i),
                               ACT.Copy).then_inc(probt_out, 1)
            act.wait_ge(pv_done, 1)
            act.activation(attn_t[:, 0:2, :].rearrange("p c t -> p (c t)"), bank(6), ACT.Copy).then_inc(attn_out, 1)

            def norm_stats(first, at):
                for b in range(TB):
                    act.wait_ge(x1_ready, first + b + 1)
                    act.activation(hfn[:, b, :], acc[:, b, :], ACT.Square,
                                   accum_out=stat(at + b)).then_inc(sq_ready, 1)
                    act.wait_ge(var_ready, first + b + 1)
                    act.activation(stat(at + 4 + b), stat(at + 2 + b), ACT.Sqrt).then_inc(sqrt_ready, 1)

            norm_stats(0, 2)
            act.wait_ge(top_ready, 1)
            for b in range(TB):
                last = act.activation(stat(72 + 4 * b, 4), stat(80 + 8 * b, 4), ACT.Exp, bias=stat(20 + b),
                                      accum_out=stat(22 + b))
            last.then_inc(gexp_ready, 1)
            act.wait_ge(gates_turned, 1)
            act.activation(gate_rows, bank(5)[0:E, 0:T], ACT.Copy).then_inc(gate_rows_ready, 1)

            def sigmoid_glu(n):
                act.wait_ge(glu_ready, n + 1)
                act.activation(sg, g_act, ACT.Sigmoid, scale=ALPHA).then_inc(sig_ready, 1)

            def evac_gu(n):
                act.wait_ge(gu_used, n * KD + KD)
                wait_pos(act, gut_done, n)
                act.activation(gu_sb[:, :], bank(0, 2), ACT.Copy).then_inc(gu_out, 1)

            def evac_sel(n):
                act.wait_ge(selt_done, n + 1)
                act.wait_ge(scat_done, 2 * n + 2)
                act.activation(sel[:, :], bank(4)[:, 0:T], ACT.Copy).then_inc(sel_ready, 1)

            def evac_y(n):
                act.wait_ge(dn_used, n * 4 + 4)
                wait_pos(act, scat_done, 2 * n + 2)
                act.activation(y_sb[:, :], bank(7), ACT.Copy).then_inc(y_ready, 1)

            def act_step(e):
                sigmoid_glu(e - 1)
                evac_gu(e)
                evac_sel(e - 1)
                evac_y(e - 1)

            evac_gu(0)
            act_step(1)
            with act.Fori(2, E) as e:
                act_step(e)
            sigmoid_glu(E - 1)
            evac_sel(E - 1)
            evac_y(E - 1)

            act.wait_ge(lists_ready, 1)
            n_extra = act.value_load(lists[0:1, 2 * N_EXTRA:2 * N_EXTRA + 1], min_val=0, max_val=N_EXTRA)
            with act.If(n_extra > 0):
                with act.Fori(0, n_extra) as i:
                    n = i + E
                    evac_sel(n)
                    evac_gu(n)
                    sigmoid_glu(n)
                    evac_y(n)

            for b in range(TB):
                act.wait_ge(pproj_done, b + 1)
                act.activation(pproj[:, b, :], bank(2 * b, 2), ACT.Copy).then_inc(pproj_out, 1)
            norm_stats(2, 8)
            for b in range(TB):
                act.wait_ge(gate_done, b + 1)
                act.activation(gate_s[:, b, :], bank(2 * b, 2), ACT.Sigmoid).then_inc(gate_out, 1)
            norm_stats(4, 14)

        @block.tensor
        def _(pe):
            def mm(o, l, r, start, stop, **kw):
                return pe.matmul(o, l, r, start=start, stop=stop, **kw)

            pe.wait_ge(consts_made, 2)
            pe.wait_ge(squared, KD)
            for c in range(KD):
                last = mm(bank(0)[:, 0:T], ones[:, :], x_sq[:, c, :], c == 0, c == KD - 1)
            last.then_inc(sumsq_done, 1)
            pe.wait_ge(s_relb, 32)
            mm(bank(1)[0:HEADS, 0:T], relb[:, :], onehot, True, True).then_inc(bias_mm, 1)

            pe.wait_ge(rms_sqrt, 1)
            pe.wait_ge(bias_copied, 1)
            for k in range(KD):
                pe.wait_ge(h_ready, k + 1)
                pe.wait_ge(s_qkvu[k], 16)
                w = ring[:, k, :]
                for j in range(12):
                    col = j * P if j < 8 else 3 * AW + (j - 8) * P
                    at = j if j < 8 else j + 4
                    mm(ps[:, at * T:(at + 1) * T], w[:, col:col + P], h_t[:, k, :], k == 0 and j % 2 == 0,
                       k == KD - 1, skip_group_check=True)
                for b in range(TB):
                    last = mm(bank(4 + b), h_t[:, k, b * P:(b + 1) * P], w[:, 2 * AW:3 * AW], k == 0, k == KD - 1)
                last.then_inc(qkvu_used, 1)

            def g_pair(i):
                if i >= 2:
                    pe.wait_ge(g_out, i - 1)
                for j in range(2):
                    for k in range(KD):
                        if i == 0:
                            pe.wait_ge(s_g[k], 16)
                        last = mm(bank(6 + i % 2)[:, j * T:(j + 1) * T],
                                  ring[:, (8 + k) % 12, (2 * i + j) * P:(2 * i + j + 1) * P], h_t[:, k, :],
                                  k == 0, k == KD - 1)
                last.then_inc(g_done, 1)

            pe.wait_ge(u_out, 2)
            g_pair(0)
            g_pair(1)
            pe.wait_ge(qkvu_out, 6)
            for c in range(4):
                for h in range(2):
                    hp, r = 4 * h + c, slice(h * DH, (h + 1) * DH)
                    last = mm(ps[:, hp * T:(hp + 1) * T], q_t[r, c, P:T], k_t[r, c, :], True, True)
            last.then_inc(scores_done, 1)
            for c in range(4):
                for h in range(2):
                    hp, r = 4 * h + c, slice(h * DH, (h + 1) * DH)
                    last = mm(ps[:, 4 * BANK + hp * P:4 * BANK + (hp + 1) * P], q_t[r, c, 0:P], k_t[r, c, 0:P],
                              True, True)
            last.then_inc(scores_done, 1)
            for i in range(2, 8):
                g_pair(i)
            pe.wait_ge(pooled_ready, 1)
            pe.wait_ge(s_pw, 16)
            for i in (8, 9):
                pe.wait_ge(g_out, i - 1)
                for j in range(2):
                    g = 2 * (i - 8) + j
                    last = mm(bank(6 + i % 2)[:, j * T:(j + 1) * T], pw_sb[:, g, :], pooled[:, g, :], True, True)
                last.then_inc(g_done, 1)
            pe.wait_ge(prob_ready, 2)
            for j in range(24):
                hp, s = divmod(j, 3)
                src = prob0[:, hp, :] if s == 2 else prob1[:, hp, s * P:(s + 1) * P]
                last = pe.transpose(ps[:, j * P:(j + 1) * P], src, ident[:, :])
                if j % 4 == 3:
                    last.then_inc(probt_done, 1)
            pe.wait_ge(g_out, 10)
            pe.wait_ge(probt_out, 6)
            for c in range(4):
                for b, kc in ((0, 0), (1, 0), (1, 1)):
                    for h in range(2):
                        hp = 4 * h + c
                        j = 3 * hp + (2 if b == 0 else kc)
                        last = mm(bank(6, 2)[h * DH:(h + 1) * DH, c * T + b * P:c * T + (b + 1) * P],
                                  v_n[:, kc, (2 * c + h) * DH:(2 * c + h + 1) * DH], prob_t[:, j, :],
                                  kc == 0, kc == b)
                if c % 2:
                    last.then_inc(pv_done, 1)
            pe.wait_ge(attn_out, 2)
            for which, src, first, done in ((0, attn_t, 0, ao_done), (1, pool2_t, 4, po_done)):
                for jj in range(4):
                    for j in range(2):
                        col = (2 * jj + j) * P
                        for k in range(4):
                            if jj == 0 and j == 0 and k % 2 == 0:
                                pe.wait_ge(s_wo[2 * which + k // 2], 16)
                            last = mm(bank(first + jj)[:, j * T:(j + 1) * T],
                                      slot2(4 + 2 * which + k // 2)[:, k % 2, col:col + P], src[:, k, :],
                                      k == 0, k == 3)
                    last.then_inc(done, 1)
            for b in range(TB):
                for n in range(2):
                    for k in range(KD):
                        if b == 0 and n == 0:
                            pe.wait_ge(merged_ready, 4 if k == 0 else k // 2 + 1)
                            pe.wait_ge(s_wout[k // 2], 16)
                        last = mm(bank(2 * b + n), merged[:, k, b * P:(b + 1) * P],
                                  slot2(8 + k // 2)[:, k % 2, n * BANK:(n + 1) * BANK], k == 0, k == KD - 1)
                last.then_inc(wout_done, 1)

            def turn_norm(first, b):
                pe.wait_ge(norm_ready, first + b + 1)
                for c in range(KD):
                    last = pe.transpose(bank(4 + 2 * b, 2)[:, c * P:(c + 1) * P], hfn[:, b, c * P:(c + 1) * P],
                                        ident[:, :])
                last.then_inc(turned, 1)

            for b in range(TB):
                turn_norm(0, b)
            pe.wait_ge(s_pack, 16)
            rw = consts[:, C_RW:C_RW + KD * E].rearrange("p (c e) -> p c e", c=KD)
            hf4 = hf_t.rearrange("p c (b t) -> p c b t", b=TB)
            for b in range(TB):
                pe.wait_ge(turned_out, b + 1)
                for c in range(KD):
                    last = mm(bank(0)[:, b * E:(b + 1) * E], hf4[:, c, b, :], rw[:, c, :], c == 0, c == KD - 1)
            last.then_inc(logits_done, 1)
            pe.wait_ge(chosen_ready, 1)
            mm(bank(2)[:, 0:E], tri[:, :], chosen[:, 0, :], True, True)
            mm(bank(2)[:, E:2 * E], ones[:, :], chosen[:, 0, :], True, False)
            mm(bank(2)[:, E:2 * E], tri[:, :], chosen[:, 1, :], False, True).then_inc(rank_done, 1)
            mm(bank(3)[0:1, 0:E], ones[:, 0:1], chosen[:, 0, :], True, False)
            mm(bank(3)[0:1, 0:E], ones[:, 0:1], chosen[:, 1, :], False, True).then_inc(count_done, 1)
            pe.wait_ge(gates_ready, 1)
            for b in range(TB):
                last = pe.transpose(bank(5)[0:E, b * P:(b + 1) * P], gates[:, b, :], ident[:, :])
            last.then_inc(gates_turned, 1)

            def gather(n, h, scattered):
                pe.wait_ge(pick_ready, n + 1)
                wait_pos(pe, added, 2 * scattered)
                for c in range(KD):
                    for b in range(TB):
                        last = mm(bank(6)[:, c * SLOTS:(c + 1) * SLOTS], hfn[:, b, c * P:(c + 1) * P],
                                  pick[:, h, b, :], b == 0, b == TB - 1)
                last.then_inc(gath_done, 1)

            def turn_sel(n, scattered):
                pe.wait_ge(pickg_ready, n + 1)
                pe.wait_ge(added, 2 * scattered)
                for b in range(TB):
                    last = pe.transpose(bank(4)[:, b * P:(b + 1) * P],
                                        pick_g[:, b, :, :].rearrange("p a s -> p (a s)"), ident[:, :])
                last.then_inc(selt_done, 1)

            def gate_up(n, h, landed):
                pe.wait_ge(xg_ready, n + 1)
                wait_pos(pe, gu_out, n)
                for k in range(KD):
                    pe.wait_ge(s_gu[h][k], landed)
                    for q in range(4):
                        half = slice(SLOTS * (q % 2), SLOTS * (q % 2 + 1))
                        last = mm(bank(q // 2)[half, :], xg[:, h, k, :], ring[:, 8 * h + k, q * BANK:(q + 1) * BANK],
                                  k == 0, k == KD - 1)
                    last.then_inc(gu_used, 1)

            def down(n, scattered, landed):
                pe.wait_ge(hid_ready, n + 1)
                wait_pos(pe, added, 2 * scattered)
                hid4 = hid.rearrange("p (b q a s) -> p b q a s", b=2, q=2, a=2)
                for u in range(4):
                    pe.wait_ge(s_dn[u], landed)
                    for j in range(2):
                        k = 2 * u + j
                        for half in range(2):
                            last = mm(bank(7)[SLOTS * half:SLOTS * (half + 1), :], hid4[:, k // 4, k % 2, k // 2 % 2, :],
                                      slot2(16 + u)[:, j, half * BANK:(half + 1) * BANK], k == 0, k == KD - 1)
                    last.then_inc(dn_used, 1)

            def turn_gu(n):
                pe.wait_ge(gu_out, n + 1)
                wait_pos(pe, gut_read, n)
                pairs = gu_sb[:, :].rearrange("p (t r k) -> p t r k", t=4, k=2)
                for kind in range(2):
                    for t in range(4):
                        last = pe.transpose(bank(2 + kind)[:, t * P:(t + 1) * P], pairs[:, t, :, kind], ident[:, :])
                last.then_inc(gut_done, 1)

            def scatter(n, scattered, gathered):
                pe.wait_ge(y_ready, n + 1)
                pe.wait_ge(sel_ready, n + 1)
                pe.wait_ge(added, 2 * scattered)
                for b in range(TB):
                    if b == 1:
                        pe.wait_ge(xg_ready, gathered)
                    for half in range(2):
                        r = slice(SLOTS * half, SLOTS * (half + 1))
                        last = mm(bank(4 + 2 * b + half), sel[r, b * P:(b + 1) * P], y_sb[r, :], True, True)
                    last.then_inc(scat_done, 1)

            gather(0, 0, 0)
            gate_up(0, 0, 16)
            gather(1, 1, 0)
            pe.wait_ge(counts_read, 1)
            turn_gu(0)
            pe.wait_ge(gate_rows_ready, 1)
            pe.wait_ge(s_bd, 32)
            pe.wait_ge(xg_ready, 2)
            for b in range(TB):
                for half in range(2):
                    last = mm(bank(4 + 2 * b + half), gate_rows[:, b * P:(b + 1) * P], bd_half[half], True, True)
                last.then_inc(scat_done, 1)

            def pe_step(e, h, gu_landed):
                gate_up(e, h, gu_landed)
                gather(e + 1, 1 - h, e)
                turn_sel(e - 1, e)
                down(e - 1, e, e * 16)
                turn_gu(e)
                scatter(e - 1, e, e + 2)

            pe_step(1, 1, 16)
            with pe.Fori(1, E // 2 - 1) as it:
                for h in range(2):
                    pe_step(2 * it + h, h, it * 16 + 16)
            pe_step(E - 2, 0, 8 * E)
            gate_up(E - 1, 1, 8 * E)
            turn_sel(E - 2, E - 1)
            down(E - 2, E - 1, 16 * (E - 1))
            turn_gu(E - 1)
            scatter(E - 2, E - 1, E)
            turn_sel(E - 1, E)
            down(E - 1, E, 16 * E)
            scatter(E - 1, E, E)

            pe.wait_ge(lists_ready, 1)
            n_extra = pe.value_load(lists[0:1, 2 * N_EXTRA:2 * N_EXTRA + 1], min_val=0, max_val=N_EXTRA)
            with pe.If(n_extra > 0):
                with pe.Fori(0, n_extra) as i:
                    n = i + E
                    gather(n, 0, n + 1)
                    turn_sel(n, n + 1)
                    gate_up(n, 0, i * 16 + (E // 2 + 1) * 16)
                    turn_gu(n)
                    down(n, n + 1, n * 16 + 16)
                    scatter(n, n + 1, n + 1)

            pe.wait_ge(s_ple_small[0], 16)
            pe.wait_ge(s_ple_small[1], 16)
            for b in range(TB):
                for n in range(2):
                    for k in range(2):
                        last = mm(bank(2 * b + n), pt_sb[:, k, b * P:(b + 1) * P], wpp[:, k, n * BANK:(n + 1) * BANK],
                                  k == 0, k == 1)
                last.then_inc(pproj_done, 1)
            for b in range(TB):
                turn_norm(2, b)
            for b in range(TB):
                pe.wait_ge(pproj_out, b + 1)
                pe.wait_ge(turned_out, 3 + b)
                for n in range(2):
                    for k in range(KD):
                        pe.wait_ge(s_ple[k // 2], 16)
                        last = mm(bank(2 * b + n), hp_t[:, k, b, :], wpg[:, k, n * BANK:(n + 1) * BANK],
                                  k == 0, k == KD - 1)
                last.then_inc(gate_done, 1)

        @block.vector
        def _(dve):
            chain = Chain(dve, dve_chain)
            tt, ts, stt = dve.tensor_tensor, dve.tensor_scalar, dve.scalar_tensor_tensor
            dve.memset(stat(0), EPS).then_inc(eps_ready, 1)
            dve.wait_ge(s_xt, 16)
            for c in range(1, KD, 2):
                tt(x_sq[:, c, :], x_raw[:, c, :], x_raw[:, c, :], ALU.mult).then_inc(squared, 1)
            dve.wait_ge(cnt_ready, 1)
            dve.reciprocal(gu_sb[:, :], gu_sb[:, :]).then_inc(inv_ready, 1)
            dve.wait_ge(rms_sqrt, 1)
            chain(dve.reciprocal(row256[:, :], row256[:, :]))
            dve.wait_ge(s_pack, 16)
            for c in range(KD):
                stt(out=h_t[:, c, :], in0=x_raw[:, c, :], scalar=consts[:, C_MIX + c:C_MIX + c + 1],
                    in1=row256[:, :], op0=ALU.mult, op1=ALU.mult).then_inc(h_ready, 1)
            dve.wait_ge(qkvu_used, KD)
            dve.tensor_copy(u_t[:, 2:4, :].rearrange("p c t -> p (c t)"), bank(7)).then_inc(u_out, 1)
            dve.tensor_copy(q_t[:, 2:4, :].rearrange("p c t -> p (c t)"), bank(1)).then_inc(qkvu_out, 1)
            dve.tensor_copy(k_t[:, 2:4, :].rearrange("p c t -> p (c t)"), bank(3)).then_inc(qkvu_out, 1)
            dve.tensor_copy(v_n[:, 1, :], bank(5)).then_inc(qkvu_out, 1)
            dve.wait_ge(s_bias_in, 32)
            for i, (prob, src, bs) in enumerate(((prob1, ps[:, 0:4 * BANK], bias),
                                                 (prob0, ps[:, 4 * BANK:6 * BANK], bias[:, :, P:T]))):
                dve.wait_ge(scores_done, i + 1)
                chain(stt(out=prob, in0=src.rearrange("p (h k) -> p h k", h=HEADS), scalar=DH ** -0.5, in1=bs,
                          op0=ALU.mult, op1=ALU.add))
                chain(dve.tensor_reduce(stat(24 + 8 * i, 8), prob, AX, ALU.max))
                ts(stat(40 + 8 * i, 8), stat(24 + 8 * i, 8), -1.0, None, ALU.mult).then_inc(max_ready, 1)
            for i, prob in enumerate((prob1, prob0)):
                dve.wait_ge(exp_done, 8 + 8 * i)
                chain(dve.reciprocal(stat(24 + 8 * i, 8), stat(56 + 8 * i, 8)))
                tt(prob, prob, stat(24 + 8 * i, 8).unsqueeze(2).to_broadcast([P, HEADS, prob.shape[2]]),
                   ALU.mult).then_inc(prob_ready, 1)
            for i in range(1, 6, 2):
                dve.wait_ge(probt_done, i + 1)
                dve.tensor_copy(prob_t[:, 4 * i:4 * i + 4, :].rearrange("p j q -> p (j q)"),
                                bank(i)).then_inc(probt_out, 1)
            dve.wait_ge(pv_done, 2)
            dve.tensor_copy(attn_t[:, 2:4, :].rearrange("p c t -> p (c t)"), bank(7)).then_inc(attn_out, 1)
            dve.wait_ge(g_out, 10)
            for jj in range(4):
                dve.wait_ge(ao_done, jj + 1)
                m = mid[:, jj * BANK:(jj + 1) * BANK]
                chain(tt(m, bank(jj), g_t[:, 2 * jj:2 * jj + 2, :].rearrange("p c t -> p (c t)"), ALU.mult))
            for jj in range(4):
                dve.wait_ge(po_done, jj + 1)
                m = mid[:, jj * BANK:(jj + 1) * BANK]
                chain(tt(branch, bank(4 + jj), g_t[:, 8 + 2 * jj:10 + 2 * jj, :].rearrange("p c t -> p (c t)"),
                         ALU.mult))
                ins = tt(m, m, branch, ALU.add)
                ins.then_inc(merged_ready, 1)
                dve.wait_ge(merged_ready, jj + 1)
            dve.wait_ge(s_x, 16)

            def norm_block(first, at, b, last_out=None):
                dve.wait_ge(sq_ready, first + b + 1)
                ts(stat(at + 2 + b), stat(at + b), 1.0 / D, EPS, ALU.mult, ALU.add).then_inc(var_ready, 1)
                dve.wait_ge(sqrt_ready, first + b + 1)
                chain(dve.reciprocal(stat(18 + b), stat(at + 4 + b)))
                if last_out is None:
                    ts(hfn[:, b, :], acc[:, b, :], stat(18 + b), None, ALU.mult).then_inc(norm_ready, 1)

            def turned_evac(first, b, col, view):
                dve.wait_ge(turned, first + b + 1)
                tt(view[:, :, b, :], bank(4 + 2 * b, 2).rearrange("p (c t) -> p c t", c=KD),
                   consts[:, col:col + KD].unsqueeze(2).to_broadcast([P, KD, P]), ALU.mult).then_inc(turned_out, 1)

            for b in range(TB):
                dve.wait_ge(wout_done, b + 1)
                tt(acc[:, b, :], acc[:, b, :], bank(2 * b, 2), ALU.add).then_inc(x1_ready, 1)
                norm_block(0, 2, b)
            hf4 = hf_t.rearrange("p c (b t) -> p c b t", b=TB)
            for b in range(TB):
                turned_evac(0, b, C_FFN, hf4)
            dve.wait_ge(logits_done, 1)
            dve.wait_ge(s_rb, 16)
            logits = rank1
            chain(tt(logits[:, :, :], bank(0)[:, 0:TB * E].rearrange("p (b e) -> p b e", b=TB),
                     rb_bc[:, :].unsqueeze(1).to_broadcast([P, TB, E]), ALU.add))
            idx = hot_g[:, 0, 0:16].bitcast(U32)
            for b in range(TB):
                chain(dve.max(stat(80 + 8 * b, 8), logits[:, b, :]))
                chain(dve.max_index(idx[:, 8 * b:8 * b + 8], stat(80 + 8 * b, 8), logits[:, b, :]))
                ins = ts(stat(20 + b), stat(80 + 8 * b), -1.0, None, ALU.mult)
            ins.then_inc(top_ready, 1)
            idx1 = hot_g[:, 1, 0:8]
            chain(dve.tensor_copy(idx1.rearrange("p (b k) -> p b k", b=TB),
                                  idx.rearrange("p (b k) -> p b k", b=TB)[:, :, 0:TOP_K]))
            chain(ts(idx1, idx1, 1.0, None, ALU.add))
            chain(tt(hot[:, :, :], iota1[:, 0:E].unsqueeze(1).to_broadcast([P, TB * TOP_K, E]),
                     idx1.unsqueeze(2).to_broadcast([P, TB * TOP_K, E]), ALU.is_equal))
            for b in range(TB):
                ins = dve.tensor_reduce(chosen[:, b, :], hot[:, TOP_K * b:TOP_K * (b + 1), :]
                                        .rearrange("p k e -> p e k"), AX, ALU.add)
            ins.then_inc(chosen_ready, 1)
            dve.wait_ge(gexp_ready, 1)
            chain(dve.reciprocal(stat(22, 2), stat(22, 2)))
            chain(tt(stat(72, 8).rearrange("p (b k) -> p b k", b=TB), stat(72, 8).rearrange("p (b k) -> p b k", b=TB),
                     stat(22, 2).unsqueeze(2).to_broadcast([P, TB, TOP_K]), ALU.mult))
            chain(tt(hot_g[:, :, :], hot[:, :, :], stat(72, 8).unsqueeze(2).to_broadcast([P, TB * TOP_K, E]), ALU.mult))
            for b in range(TB):
                ins = dve.tensor_reduce(gates[:, b, :], hot_g[:, TOP_K * b:TOP_K * (b + 1), :]
                                        .rearrange("p k e -> p e k"), AX, ALU.add)
            ins.then_inc(gates_ready, 1)
            dve.wait_ge(gates_ready, 1)
            dve.wait_ge(rank_done, 1)
            chain(stt(out=rank1[:, :, :], in0=bank(2)[:, 0:TB * E].rearrange("p (b e) -> p b e", b=TB), scalar=1.0,
                      in1=chosen[:, :, :], op0=ALU.add, op1=ALU.mult))

            def column(table, e):
                one = table[:, :, e:e + 1] if isinstance(e, int) else table[:, :, bass.ds(e, 1)]
                return one.to_broadcast([P, TB, SLOTS])

            def make_pick(n, h, e, gathered, first=0):
                wait_pos(dve, gath_done, gathered)
                slots = iota1[:, 0:SLOTS] if isinstance(first, int) else iota1[:, bass.ds(first, SLOTS)]
                tt(pick[:, h, :, :], slots.unsqueeze(1).to_broadcast([P, TB, SLOTS]), column(rank1, e),
                   ALU.is_equal).then_inc(pick_ready, 1)

            def make_pick_g(n, h, e):
                wait_pos(dve, selt_done, n)
                dve.wait_ge(pick_ready, n + 1)
                for a in range(2):
                    ins = tt(pick_g[:, :, a, :], pick[:, h, :, :], column(gates, e), ALU.mult)
                ins.then_inc(pickg_ready, 1)

            def xg_evac(n, h, served):
                dve.wait_ge(gath_done, n + 1)
                wait_pos(dve, gu_used, served * KD)
                tt(xg[:, h, :, :], bank(6).rearrange("p (c s) -> p c s", c=KD),
                   consts[:, C_FFN:C_FFN + KD].unsqueeze(2).to_broadcast([P, KD, SLOTS]),
                   ALU.mult).then_inc(xg_ready, 1)

            bgu = consts[:, C_BGU:C_BGU + 16 * E].rearrange("p (e k t) -> p e k t", e=E, k=2)

            def expert_bias(e, kind):
                one = bgu[:, e, kind, :] if isinstance(e, int) else \
                    bgu[:, bass.ds(e, 1), kind, :].rearrange("p o t -> p (o t)")
                return one.unsqueeze(2).to_broadcast([P, 8, SLOTS])

            def swiglu(n, e):
                def tiles(x):
                    return x.rearrange("p (t s) -> p t s", s=SLOTS)
                dve.wait_ge(gut_done, n + 1)
                chain(tt(tiles(g_act), tiles(bank(2)), expert_bias(e, 0), ALU.add))
                ts(g_act, g_act, LIMIT, None, ALU.min).then_inc(glu_ready, 1)
                tt(tiles(l_act), tiles(bank(3)), expert_bias(e, 1), ALU.add).then_inc(gut_read, 1)
                dve.wait_ge(gut_read, n + 1)
                chain(ts(l_act, l_act, LIMIT, -LIMIT, ALU.min, ALU.max))
                dve.wait_ge(glu_ready, n + 1)
                chain(stt(out=l_act, in0=l_act, scalar=1.0, in1=g_act, op0=ALU.add, op1=ALU.mult))
                dve.wait_ge(sig_ready, n + 1)
                wait_pos(dve, dn_used, n * 4)
                dve.wait_ge(scat_done, 2)
                tt(hid, l_act, sg, ALU.mult).then_inc(hid_ready, 1)

            def add_back(j):
                for b in range(TB):
                    dve.wait_ge(scat_done, 2 * j + b + 1)
                    tt(acc[:, b, :], acc[:, b, :], bank(4 + 2 * b, 2), ALU.add).then_inc(added, 1)

            make_pick(0, 0, 0, 0)
            xg_evac(0, 0, 0)
            make_pick_g(0, 0, 0)
            dve.wait_ge(count_done, 1)
            flat = hot[0:1, :, :].rearrange("p a e -> p (a e)")
            has, place = flat[:, 0:3 * E], flat[:, 3 * E:6 * E]
            picked = hot_g[0:1, :, :].rearrange("p a e -> p (a e)")[:, 0:3 * E].rearrange("p (b e) -> p b e", b=3)
            place3 = place.rearrange("p (b e) -> p b e", b=3)
            sums = small[0:1, 24:24 + 2 * N_EXTRA + 1]
            for b in range(3):
                ins = ts(has[:, b * E:(b + 1) * E], bank(3)[0:1, 0:E], float(SLOTS * (b + 1)), None, ALU.is_gt)
            ins.then_inc(counts_read, 1)
            dve.wait_ge(counts_read, 1)
            chain(dve.tensor_tensor_scan(place, ones[0:1, 0:3 * E], has, 0.0, ALU.mult, ALU.add))
            chain(tt(place, place, has, ALU.mult))
            experts = iota1[0:1, 0:E].unsqueeze(1).to_broadcast([1, 3, E])
            blocks = iota1[0:1, 0:3].unsqueeze(2).to_broadcast([1, 3, E])
            for i in range(N_EXTRA):
                for j, code in enumerate((experts, blocks)):
                    chain(stt(out=picked, in0=place3, scalar=float(i + 1), in1=code, op0=ALU.is_equal,
                              op1=ALU.mult, accum_out=sums[:, j * N_EXTRA + i:j * N_EXTRA + i + 1]))
            chain(dve.tensor_reduce(sums[:, 2 * N_EXTRA:], has, AX, ALU.add))
            chain(ts(sums[:, 0:N_EXTRA], sums[:, 0:N_EXTRA], -1.0, 0.0, ALU.add, ALU.max))
            chain(ts(sums[:, N_EXTRA:2 * N_EXTRA], sums[:, N_EXTRA:2 * N_EXTRA], float(SLOTS), None, ALU.mult))
            dve.tensor_copy(lists[:, :], sums).then_inc(lists_ready, 1)

            make_pick(1, 1, 1, 0)
            xg_evac(1, 1, 0)

            def dve_step(e, h):
                swiglu(e - 1, e - 1)
                add_back(e - 1)
                make_pick(e + 1, 1 - h, e + 1, e)
                xg_evac(e + 1, 1 - h, e)
                make_pick_g(e, h, e)

            dve_step(1, 1)
            steps = 3
            start = chain.n
            with dve.Fori(1, E // 2 - 1) as it:
                for h in range(2):
                    chain.n = (it - 1) * (2 * steps) + (start + h * steps)
                    dve_step(2 * it + h, h)
            chain.n = start + steps * (E - 4)
            dve_step(E - 2, 0)
            swiglu(E - 2, E - 2)
            add_back(E - 2)
            make_pick_g(E - 1, 1, E - 1)
            swiglu(E - 1, E - 1)
            add_back(E - 1)
            add_back(E)
            dve.wait_ge(added, 2 * E + 2)
            start = chain.n

            n_extra = dve.value_load(lists[0:1, 2 * N_EXTRA:2 * N_EXTRA + 1], min_val=0, max_val=N_EXTRA)
            with dve.If(n_extra > 0):
                with dve.Fori(0, n_extra) as i:
                    n = i + E
                    e = dve.value_load(lists[0:1, bass.ds(i, 1)], min_val=0, max_val=E - 1)
                    first = dve.value_load(lists[0:1, bass.ds(i + N_EXTRA, 1)], min_val=0, max_val=T - SLOTS)
                    chain.n = i * steps + start
                    make_pick(n, 0, e, n, first)
                    make_pick_g(n, 0, e)
                    xg_evac(n, 0, n)
                    swiglu(n, e)
                    add_back(n + 1)
                    dve.wait_ge(added, 2 * n + 4)
            chain = Chain(dve, dve_tail_chain)

            def tail_norm(first, at, b, final):
                dve.wait_ge(sq_ready, first + b + 1)
                ts(stat(at + 2 + b), stat(at + b), 1.0 / D, EPS, ALU.mult, ALU.add).then_inc(var_ready, 1)
                dve.wait_ge(sqrt_ready, first + b + 1)
                chain(dve.reciprocal(stat(20 + b), stat(at + 4 + b)))
                if not final:
                    ts(hfn[:, b, :], acc[:, b, :], stat(20 + b), None, ALU.mult).then_inc(norm_ready, 1)
                else:
                    stt(out=acc[:, b, :], in0=acc[:, b, :], scalar=stat(20 + b), in1=fg_bc, op0=ALU.mult,
                        op1=ALU.mult).then_inc(fin_ready, 1)

            for b in range(TB):
                dve.memset(stat(b), 0.0).then_inc(x1_ready, 1)
            for b in range(TB):
                tail_norm(2, 8, b, False)
            for b in range(TB):
                turned_evac(2, b, C_PLE, hp_t)
            dve.wait_ge(s_ple_small[2], 16)
            for b in range(TB):
                dve.wait_ge(gate_out, b + 1)
                chain(tt(gate_s[:, b, :], gate_s[:, b, :], pproj[:, b, :], ALU.mult))
                tt(acc[:, b, :], acc[:, b, :], gate_s[:, b, :], ALU.add).then_inc(x1_ready, 1)
            for b in range(TB):
                tail_norm(4, 14, b, True)


def kernel(**inputs):
    from concourse import bacc
    from concourse.bass_utils import run_bass_kernel_spmd

    def f(name, *shape):
        return np.ascontiguousarray(inputs[name]).reshape(shape)

    columns = [f(n, -1, P).T for n in ("norm_mix_g", "norm_ffn_g", "norm_ple_g", "pool_scale")]
    router = f("router_w", KD, P, E).transpose(1, 0, 2).reshape(P, KD * E)
    bgu = f("b_gate_up", E, 2, 2, 2, P, 2).transpose(4, 0, 5, 1, 3, 2).reshape(P, E * 16)
    dist = T - 1 - np.arange(T)
    exact = BUCKETS // 2
    large = exact + (np.log(np.maximum(dist, 1) / exact) / math.log(MAX_DISTANCE / exact) * exact).astype(int)
    bucket = np.where(dist < exact, dist, np.minimum(large, BUCKETS - 1))
    arrays = {
        "x": f("x", T, D), "x_t": np.ascontiguousarray(f("x", T, D).T),
        "p_t": np.ascontiguousarray(f("p", T, PLE).T),
        "pack": np.ascontiguousarray(np.concatenate(columns + [router, bgu], axis=1)),
        "rel_bias": f("rel_bias", BUCKETS, HEADS),
        "bucket_of": (np.arange(BUCKETS)[:, None] == bucket[None, :]).astype(np.float32),
        "w_in": f("w_in", D, 2 * NW), "pool_w": f("pool_w", GROUPS, P, P),
        "w_o_attn": f("w_o_attn", AW, D), "w_o_pool": f("w_o_pool", AW, D), "w_out": f("w_out", D, D),
        "router_b": f("router_b", E), "w_gate_up": f("w_gate_up", E, D, NW), "w_down": f("w_down", E, D, D),
        "b_down": f("b_down", E, D), "w_ple_gate": f("w_ple_gate", D, D), "w_ple_proj": f("w_ple_proj", PLE, D),
        "norm_final_g": f("norm_final_g", D),
    }
    nc = bacc.Bacc("TRN2", target_bir_lowering=False, num_devices=1)
    args = {n: nc.dram_tensor(f"in_{n}", a.shape, mybir.dt.from_np(a.dtype), kind="ExternalInput").ap()
            for n, a in arrays.items()}
    out = nc.dram_tensor("out_0", (T, D), F32, kind="ExternalOutput").ap()
    block_kernel(nc, **args, out=out)
    r = run_bass_kernel_spmd(nc, [{f"in_{n}": a for n, a in arrays.items()}], core_ids=[0])
    return r.results[0]["out_0"].reshape(1, T, D)
```

```python
import math
from contextlib import ExitStack

import numpy as np

import concourse.bass as bass
from concourse import mybir

P = 128
D = 1024
T = 256
TB = T // P
KD = D // P
HEADS = 8
DH = 64
AW = HEADS * DH
NW = 2 * D
BUCKETS = 32
MAX_DISTANCE = 128
WINDOWS = (2, 4, 8, 16)
GROUPS = len(WINDOWS)
E = 32
TOP_K = 4
SLOTS = 64
N_EXTRA = 16
LIMIT = 7.0
ALPHA = 1.702
PLE = 256
EPS = 1e-6
NEG = -3.0e38
BANK = 512

C_MIX, C_FFN, C_PLE, C_POOL, C_RW, C_BGU = 0, 8, 16, 24, 28, 28 + KD * E
N_PACK = C_BGU + E * 16

ALU = mybir.AluOpType
ACT = mybir.ActivationFunctionType
AX = mybir.AxisListType.X
F32 = mybir.dt.float32
I32 = mybir.dt.int32
U32 = mybir.dt.uint32


class Chain:

    def __init__(self, eng, sem):
        self.eng, self.sem, self.n = eng, sem, 0

    def __call__(self, ins):
        ins.then_inc(self.sem, 1)
        self.n = self.n + 1
        self.eng.wait_ge(self.sem, self.n)


def wait_pos(eng, sem, value):
    if not isinstance(value, int) or value > 0:
        eng.wait_ge(sem, value)


def block_kernel(nc, x, x_t, p_t, pack, rel_bias, bucket_of, w_in, pool_w, w_o_attn, w_o_pool, w_out,
                 router_b, w_gate_up, w_down, b_down, w_ple_gate, w_ple_proj, norm_final_g, out):
    ctx = ExitStack()
    with ctx:
        def sb(name, shape, dt=F32):
            return ctx.enter_context(nc.sbuf_tensor(name, shape, dt))

        def sem(name):
            return ctx.enter_context(nc.semaphore(name))

        bias_rows = nc.dram_tensor("bias_rows", (HEADS, P, 384), F32).ap()

        ring = sb("ring", [P, 20, NW])
        acc = sb("acc", [P, TB, D])
        hfn = sb("hfn", [P, TB, D])
        mid = sb("mid", [P, 2048])
        consts = sb("consts", [P, N_PACK])
        xg = sb("xg", [P, 2, KD, SLOTS])
        gu_sb = sb("gu_sb", [P, 2 * BANK])
        y_sb = sb("y_sb", [P, BANK])
        sel = sb("sel", [P, T])
        pick = sb("pick", [P, 2, TB, SLOTS])
        pick_g = sb("pick_g", [P, TB, 2, SLOTS])
        spare = sb("spare", [P, BANK])
        chosen = sb("chosen", [P, TB, E])
        gates = sb("gates", [P, TB, E])
        rank1 = sb("rank1", [P, TB, E])
        small = sb("small", [P, 96])
        iota1 = sb("iota1", [P, T])
        ident = sb("ident", [P, P])
        tri = sb("tri", [P, P])
        ones = sb("ones", [P, P])
        relb = sb("relb", [BUCKETS, HEADS])
        row256 = sb("row256", [P, T])
        rb_bc = sb("rb_bc", [P, E])
        lists = sb("lists", [1, 2 * N_EXTRA + 1], I32)

        hot = spare[:, 0:256].rearrange("p (k e) -> p k e", e=E)
        hot_g = spare[:, 256:512].rearrange("p (k e) -> p k e", e=E)

        h_t = ring[:, 12, :].rearrange("p (c t) -> p c t", c=KD)
        q_t = ring[:, 13, 0:1024].rearrange("p (c t) -> p c t", c=4)
        k_t = ring[:, 13, 1024:2048].rearrange("p (c t) -> p c t", c=4)
        v_n = ring[:, 14, 0:1024].rearrange("p (b n) -> p b n", b=TB)
        u_t = ring[:, 14, 1024:2048].rearrange("p (g t) -> p g t", g=GROUPS)
        g_t = ring[:, 15:17, :].rearrange("p s n -> p (s n)").rearrange("p (c t) -> p c t", t=T)
        bias = ring[:, 17, :].rearrange("p (h k) -> p h k", h=HEADS)
        pool2_t = ring[:, 17, 0:1024].rearrange("p (g t) -> p g t", g=GROUPS)
        prob1 = ring[:, 18, :].rearrange("p (h k) -> p h k", h=HEADS)
        prob0 = ring[:, 19, 0:1024].rearrange("p (h k) -> p h k", h=HEADS)
        attn_t = ring[:, 19, 1024:2048].rearrange("p (c t) -> p c t", c=4)
        prob_t = ring[:, 12:14, :].rearrange("p s n -> p (s n)")[:, 0:24 * P].rearrange("p (j q) -> p j q", q=P)
        x_raw = ring[:, 18, :].rearrange("p (c t) -> p c t", c=KD)
        x_sq = ring[:, 16, :].rearrange("p (c t) -> p c t", c=KD)
        x_ss = mid[:, 0:T]
        win_a = hfn[:, 0, :].rearrange("p (g t) -> p g t", g=GROUPS)
        win_b = hfn[:, 1, :].rearrange("p (g t) -> p g t", g=GROUPS)
        inv_cnt = gu_sb[:, :].rearrange("p (g t) -> p g t", g=GROUPS)
        pooled = xg[:, :, :, :].rearrange("p a c s -> p (a c s)").rearrange("p (g t) -> p g t", g=GROUPS)
        branch = xg[:, 0, :, :].rearrange("p c s -> p (c s)")
        pw_sb = y_sb[:, :].rearrange("p (g d) -> p g d", g=GROUPS)
        onehot = spare[0:BUCKETS, 0:T]
        bias_v = xg[0:HEADS, :, :, :].rearrange("p a c s -> p (a c s)")[:, 0:384]
        merged = mid[:, :].rearrange("p (c t) -> p c t", c=KD)
        hf_t = [x[:, 0:KD * P].rearrange("p (c t) -> p c t", c=KD) for x in (gu_sb, mid)]
        gate_rows = row256[0:E, :]
        lt_sb = pick[:, :, :, :].rearrange("p h b s -> p h (b s)")
        g_act, l_act, sg, hid = (mid[:, i * BANK:(i + 1) * BANK] for i in range(4))
        bd_half = (y_sb[0:E, :], hid[0:E, :])
        wpg = ring[:, 16:20, :].rearrange("p s (j n) -> p (s j) n", j=2)
        wpp = ring[:, 4, :].rearrange("p (j n) -> p j n", j=2)
        pt_sb = ring[:, 5, 0:512].rearrange("p (j t) -> p j t", j=2)
        fg_bc = ring[:, 5, 1024:2048]
        pproj = ring[:, 6, :].rearrange("p (b n) -> p b n", b=TB)
        gate_s = ring[:, 7, :].rearrange("p (b n) -> p b n", b=TB)
        hp_t = mid[:, :].rearrange("p (c b t) -> p c b t", c=KD, b=TB)

        def stat(a, n=1):
            return small[:, a:a + n]

        ps = ctx.enter_context(nc.psum_tensor("ps", [P, 8 * BANK], F32))

        def bank(b, n=1):
            return ps[:, b * BANK:(b + n) * BANK]

        s_xt = [sem(f"xt_landed{i}") for i in range(2)]
        s_norms, s_pack, s_pw, s_x, s_relb, s_rb, s_bd = (sem(n) for n in (
            "norms_landed", "pack_landed", "pool_w_landed", "x_landed", "rel_landed", "router_b_landed",
            "b_down_landed"))
        s_bias_out, s_bias_in = sem("bias_rows_stored"), sem("bias_landed")
        s_qkvu = [sem(f"qkvu_landed{k}") for k in range(KD)]
        s_g = [sem(f"g_landed{k}") for k in range(KD)]
        s_wo = [sem(f"{n}_landed") for n in ("w_o_pool", "w_o_attn")]
        s_wout = [sem(f"wout_landed{i}") for i in range(2)]
        s_gu = [[sem(f"gu_landed{h}_{k}") for k in range(KD)] for h in range(2)]
        s_dn = [sem(f"down_landed{u}") for u in range(4)]
        s_dn_last = [sem(f"late_down_landed{u}") for u in range(4)]
        s_ple_proj, s_fg = sem("ple_proj_landed"), sem("final_g_landed")
        s_out = sem("out_stored")

        consts_made, eps_ready = sem("consts_made"), sem("eps_ready")
        dve_chain, dve_tail_chain, pool_chain = sem("dve_chain"), sem("dve_tail_chain"), sem("pool_chain")
        squared, squares_added = sem("squared"), sem("squares_added")
        sumsq_done = sem("sumsq_done")
        rms_sqrt, row_ready, row_turned, col_ready = (sem(n) for n in (
            "rms_sqrt", "rstd_row_ready", "rstd_row_turned", "rstd_column_ready"))
        h_ready = [sem(f"h_ready{c}") for c in range(KD)]
        v_done, v_out = sem("v_done"), sem("v_evacuated")
        bias_mm, bias_copied = sem("bias_mm"), sem("bias_copied")
        qkvu_used, qkvu_out = sem("qkvu_used"), sem("qkvu_evacuated")
        u_out = sem("u_evacuated")
        g_done, g_scaled, g_out = sem("g_done"), sem("g_scaled"), sem("gates_ready_or_pooled")
        cnt_ready, inv_ready, pooled_ready = sem("cnt_ready"), sem("inv_ready"), sem("pooled_ready")
        scores_done, max_ready, exp_done, prob_ready = (sem(n) for n in (
            "scores_done", "max_ready", "exp_done", "prob_ready"))
        probt_done, probt_out = sem("prob_t_done"), sem("prob_t_evacuated")
        pv_done, attn_out = sem("pv_done"), sem("attn_evacuated")
        ao_done, po_done, merged_ready = sem("attn_branch_done"), sem("pool_branch_done"), sem("merged_ready")
        wout_done, wout_used, x1_ready = sem("wout_done"), sem("wout_used"), sem("x1_ready")
        half_mean, x2_ready = sem("half_mean_ready"), sem("x2_ready")
        sq_ready, sqrt_ready, rstd_ready, norm_ready = (sem(n) for n in (
            "sumsq_ready", "sqrt_ready", "rstd_ready", "norm_ready"))
        turned, turned_out = sem("x_turned"), sem("x_turned_evacuated")
        logits_mm, logits_out = sem("logits_product"), sem("logits_evacuated")
        logits_done, top_ready, gexp_ready, chosen_ready, gates_ready = (sem(n) for n in (
            "logits_done", "top_ready", "gate_exp_ready", "chosen_ready", "gates_ready"))
        rank_done, rank_ready, count_done, gates_turned, gate_rows_ready = (sem(n) for n in (
            "rank_done", "rank_ready", "count_done", "gates_turned", "gate_rows_ready"))
        counts_read, lists_ready = sem("counts_read"), sem("lists_ready")
        pick_ready, gath_done, xg_ready = sem("pick_ready"), sem("gather_done"), sem("xg_ready")
        xn_ready, xt_done = sem("gathered_evacuated"), sem("gathered_turned")
        pickg_ready, selt_done, sel_ready = sem("pick_g_ready"), sem("sel_turned"), sem("sel_ready")
        gu_used, gu_out, gut_done, gut_read = (sem(n) for n in (
            "gu_used", "gu_evacuated", "gu_turned", "gu_turned_read"))
        glu_ready, sig_ready, hid_ready = sem("glu_ready"), sem("sigmoid_ready"), sem("hid_ready")
        dn_used, y_ready, scat_done, added = (sem(n) for n in ("down_used", "y_ready", "scatter_done", "added"))
        pproj_done, pproj_out = sem("ple_proj_done"), sem("ple_proj_evacuated")
        fin_sq, fin_sum, fin_sqrt, fin_rstd = (sem(n) for n in (
            "final_squares", "final_sum", "final_sqrt", "final_rstd"))
        gate_done, gate_out, x3_ready, fin_ready = (sem(n) for n in (
            "ple_gate_done", "ple_gate_sigmoid", "x3_ready", "final_ready"))

        block = ctx.enter_context(nc.Block())

        wo_units = [(w_o_pool, 0), (w_o_pool, 1), (w_o_attn, 0), (w_o_attn, 1)]

        def two_chunks(w, u):
            return w[2 * u * P:(2 * u + 2) * P, :].rearrange("(j p) n -> p j n", p=P)

        def slot2(s):
            return ring[:, s, :].rearrange("p (j n) -> p j n", j=2)

        @block.sync
        def _(sp):
            def load_gu(e, h, k, landed):
                src = w_gate_up[e] if isinstance(e, int) else w_gate_up[bass.ds(e, 1)].rearrange("o d f -> (o d) f")
                sp.dma_start(ring[:, 8 * h + k, :], src[k * P:(k + 1) * P, :]).then_inc(landed, 16)

            def load_down(e, u, landed):
                src = w_down[e] if isinstance(e, int) else w_down[bass.ds(e, 1)].rearrange("o d f -> (o d) f")
                sp.dma_start(slot2(16 + u), two_chunks(src, u)).then_inc(landed, 16)

            for k in range(KD):
                if k < 2:
                    sp.dma_start(x_raw[:, 4 * k:4 * k + 4, :], x_t[4 * k * P:4 * (k + 1) * P, :]
                                 .rearrange("(c p) t -> p c t", p=P)).then_inc(s_xt[k], 16)
                sp.dma_start(ring[:, k, :], w_in[k * P:(k + 1) * P, 0:NW]).then_inc(s_qkvu[k], 16)
            sp.dma_start(consts[:, C_RW:], pack[:, C_RW:]).then_inc(s_pack, 16)
            sp.dma_start(pw_sb, pool_w.rearrange("g c d -> c g d")).then_inc(s_pw, 16)
            sp.dma_start(acc[:, :, :], x.rearrange("(b p) d -> p b d", p=P)).then_inc(s_x, 16)
            sp.dma_start(rb_bc[:, :], router_b.partition_broadcast(P)).then_inc(s_rb, 16)
            for k in range(KD):
                if k >= 4:
                    sp.wait_ge(v_done, k - 3)
                sp.dma_start(ring[:, (8 + k) % 12, :], w_in[k * P:(k + 1) * P, NW:2 * NW]).then_inc(s_g[k], 16)
            for i, (w, u) in enumerate(wo_units):
                sp.wait_ge(v_done, 5 + i)
                sp.dma_start(slot2(4 + i), two_chunks(w, u)).then_inc(s_wo[i // 2], 16)
            sp.wait_ge(g_done, 8)
            for i in range(4):
                sp.dma_start(slot2(8 + i), two_chunks(w_out, i)).then_inc(s_wout[i // 2], 16)
            for k in range(4):
                load_gu(0, 0, k, s_gu[0][k])
            sp.wait_ge(pv_done, 2)
            for k in (4, 5, 6):
                load_gu(1, 1, k, s_gu[1][k])
            load_down(0, 2, s_dn[2])
            for k in range(4, KD):
                sp.wait_ge(po_done if k < 6 else ao_done, 4)
                load_gu(0, 0, k, s_gu[0][k])
            sp.wait_ge(merged_ready, 4)
            for u in (0, 1, 3):
                load_down(0, u, s_dn[u])
            load_gu(1, 1, 7, s_gu[1][7])
            for k in range(4):
                sp.wait_ge(wout_used, k + 1)
                load_gu(1, 1, k, s_gu[1][k])

            sp.wait_ge(g_done, 10)
            sp.wait_ge(logits_mm, 2)
            for half in range(2):
                sp.dma_start(bd_half[half], b_down[:, half * BANK:(half + 1) * BANK]).then_inc(s_bd, 16)

            def next_gu(e, h, chunks=range(KD)):
                for k in chunks:
                    sp.wait_ge(gu_used, (e - 2) * KD + k + 1)
                    load_gu(e, h, k, s_gu[h][k])

            def next_down(e):
                for u in range(4):
                    sp.wait_ge(dn_used, (e - 1) * 4 + u + 1)
                    load_down(e, u, s_dn[u])

            GU_FIRST = 2

            def next_both(e, h):
                next_gu(e, h, range(GU_FIRST))
                next_down(e - 2)
                next_gu(e, h, range(GU_FIRST, KD))

            next_gu(2, 0)
            next_gu(3, 1)
            next_down(1)
            with sp.Fori(2, E // 2) as it:
                for h in range(2):
                    next_both(2 * it + h, h)
            sp.wait_ge(gu_used, (E - 1) * KD)
            next_down(E - 2)
            for u in range(4):
                sp.dma_start(slot2(u), two_chunks(w_down[E - 1], u)).then_inc(s_dn_last[u], 16)
            sp.dma_start(pt_sb, p_t.rearrange("(j p) t -> p j t", p=P)).then_inc(s_ple_proj, 16)
            sp.dma_start(wpp, w_ple_proj.rearrange("(j p) n -> p j n", p=P)).then_inc(s_ple_proj, 16)
            for u in range(4):
                sp.wait_ge(dn_used, (E - 2) * 4 + u + 1)
                sp.dma_start(slot2(16 + u), two_chunks(w_ple_gate, u)).then_inc(s_dn[u], 16)
            sp.dma_start(fg_bc, norm_final_g.partition_broadcast(P)).then_inc(s_fg, 16)

            sp.wait_ge(lists_ready, 1)
            n_extra = sp.value_load(lists[0:1, 2 * N_EXTRA:2 * N_EXTRA + 1], min_val=0, max_val=N_EXTRA)
            with sp.If(n_extra > 0):
                with sp.Fori(0, n_extra) as i:
                    e = sp.value_load(lists[0:1, bass.ds(i, 1)], min_val=0, max_val=E - 1)
                    sp.wait_ge(gu_used, (i + E) * KD)
                    for k in range(KD):
                        load_gu(e, 1, k, s_gu[1][k])
                    sp.wait_ge(dn_used, (i + E) * 4)
                    for u in range(4):
                        src = w_down[bass.ds(e, 1)].rearrange("o d f -> (o d) f")
                        sp.dma_start(slot2(u), two_chunks(src, u)).then_inc(s_dn_last[u], 16)

            for b in range(TB):
                sp.wait_ge(fin_ready, 2 * b + 2)
                sp.dma_start(out[b * P:(b + 1) * P, :], gate_s[:, b, :]).then_inc(s_out, 16)
            sp.wait_ge(s_out, 32)

        @block.gpsimd
        def _(pool):
            chain = Chain(pool, pool_chain)
            pool.memset(ones[:, :], 1.0).then_inc(consts_made, 1)
            chain(pool.memset(ident[:, :], 0.0))
            chain(pool.affine_select(out=ident[:, :], in_=ident[:, :], compare_op=ALU.not_equal, fill=1.0,
                                     base=0, pattern=[[-1, P]], channel_multiplier=1))
            pool.wait_ge(consts_made, 1)
            chain(pool.affine_select(out=tri[:, :], in_=ones[:, :], compare_op=ALU.is_gt, fill=0.0,
                                     base=0, pattern=[[1, P]], channel_multiplier=-1))
            chain(pool.iota(iota1[:, :], pattern=[[1, T]], base=1, channel_multiplier=0,
                            allow_small_or_imprecise_dtypes=True))
            pool.memset(bias_v[:, 256:384], NEG).then_inc(consts_made, 1)
            for g, w in enumerate(WINDOWS):
                last = pool.tensor_scalar(inv_cnt[:, g, :], iota1[:, :], float(w), None, ALU.min)
            last.then_inc(cnt_ready, 1)

            pool.wait_ge(u_out, 2)
            pool.wait_ge(s_bias_out, 16)
            src = u_t
            for j in range(GROUPS):
                dst = (win_a, win_b)[j % 2]
                sh = 1 << j
                pool.tensor_copy(dst[:, j:, 0:sh], src[:, j:, 0:sh])
                chain(pool.tensor_tensor(dst[:, j:, sh:], src[:, j:, sh:], src[:, j:, 0:T - sh], ALU.add))
                if j == 0:
                    pool.wait_ge(inv_ready, 1)
                chain(pool.tensor_tensor(pooled[:, j, :], dst[:, j, :], inv_cnt[:, j, :], ALU.mult))
                last = pool.tensor_tensor(pooled[:, j, :], pooled[:, j, :], u_t[:, j, :], ALU.subtract)
                src = dst
            last.then_inc(pooled_ready, 1)

        @block.scalar
        def _(act):
            act.dma_start(consts[:, 0:C_RW], pack[:, 0:C_RW]).then_inc(s_norms, 16)
            act.dma_start(relb[:, :], rel_bias).then_inc(s_relb, 16)
            act.dma_start(onehot, bucket_of).then_inc(s_relb, 16)
            act.wait_ge(s_norms, 16)
            for c in range(0, KD, 2):
                act.wait_ge(s_xt[c // 4], 16)
                act.activation(h_t[:, c, :], x_raw[:, c, :], ACT.Copy,
                               scale=consts[:, C_MIX + c:C_MIX + c + 1]).then_inc(h_ready[c], 1)
            for c in range(0, KD, 2):
                act.activation(x_sq[:, c, :], x_raw[:, c, :], ACT.Square).then_inc(squared, 1)
            act.wait_ge(sumsq_done, 1)
            act.wait_ge(eps_ready, 1)
            act.activation(row256[:, :], bank(4)[:, 0:T], ACT.Sqrt, bias=stat(0), scale=1.0 / D).then_inc(rms_sqrt, 1)
            act.wait_ge(bias_mm, 1)
            act.wait_ge(consts_made, 2)
            act.activation(bias_v[:, 0:256], bank(5)[0:HEADS, 0:256], ACT.Copy).then_inc(bias_copied, 1)
            act.wait_ge(bias_copied, 1)
            act.dma_start(bias_rows[:, :, :], bias_v.unsqueeze(1).to_broadcast([HEADS, P, 384])).then_inc(s_bias_out, 16)
            act.wait_ge(s_bias_out, 16)
            for par in range(2):
                src = bass.AP(tensor=bias_rows.tensor, offset=par * P * 384 + P - 1,
                              ap=[[384 - 1, P], [2 * P * 384, 4], [1, T]])
                act.dma_start(bias[:, 4 * par:4 * par + 4, :], src).then_inc(s_bias_in, 16)
            act.wait_ge(v_done, KD)
            act.wait_ge(col_ready, 1)
            for b in range(TB):
                act.activation(v_n[:, b, :], bank(4 + b), ACT.Copy, scale=stat(2 + b)).then_inc(v_out, 1)

            def g_sigmoid(i):
                act.wait_ge(g_scaled, i + 1)
                g2 = g_t[:, 2 * i:2 * i + 2, :].rearrange("p c t -> p (c t)")
                act.activation(g2, g2, ACT.Sigmoid).then_inc(g_out, 1)

            g_sigmoid(0)
            g_sigmoid(1)
            act.wait_ge(max_ready, 1)
            for h in range(HEADS):
                act.activation(prob1[:, h, :], prob1[:, h, :], ACT.Exp, bias=stat(40 + h),
                               accum_out=stat(56 + h)).then_inc(exp_done, 1)
            act.wait_ge(max_ready, 2)
            for h in range(HEADS):
                act.activation(prob0[:, h, :], prob0[:, h, :], ACT.Exp, bias=stat(48 + h),
                               accum_out=stat(64 + h)).then_inc(exp_done, 1)
            for i in range(2, 8):
                g_sigmoid(i)
            for i in (8, 9):
                act.wait_ge(g_done, i + 1)
                for j in range(2):
                    g = 2 * (i - 8) + j
                    last = act.activation(pool2_t[:, g, :], bank(6 + i % 2)[:, j * T:(j + 1) * T], ACT.Copy,
                                          scale=consts[:, C_POOL + g:C_POOL + g + 1])
                last.then_inc(g_out, 1)
            for i in range(0, 6, 2):
                act.wait_ge(probt_done, i + 1)
                act.activation(prob_t[:, 4 * i:4 * i + 4, :].rearrange("p j q -> p (j q)"), bank(i),
                               ACT.Copy).then_inc(probt_out, 1)
            act.wait_ge(pv_done, 1)
            act.activation(attn_t[:, 0:2, :].rearrange("p c t -> p (c t)"), bank(6), ACT.Copy).then_inc(attn_out, 1)

            def squares(b, cols, at):
                act.activation(hfn[:, b, cols], acc[:, b, cols], ACT.Square, accum_out=stat(at)).then_inc(sq_ready, 1)

            def root(b, of, bias):
                act.activation(stat(10 + b), stat(of), ACT.Sqrt, bias=stat(bias), scale=1.0 / D).then_inc(sqrt_ready, 1)

            def normed(b):
                act.wait_ge(rstd_ready, b + 1)
                act.activation(hfn[:, b, :], acc[:, b, :], ACT.Copy, scale=stat(12 + b)).then_inc(norm_ready, 1)

            def logits_evac(b):
                act.wait_ge(logits_mm, b + 1)
                act.activation(lt_sb[:, b, :], bank(b)[:, 0:P], ACT.Copy).then_inc(logits_out, 1)

            act.wait_ge(x1_ready, 1)
            squares(0, slice(0, D), 8)
            act.wait_ge(sq_ready, 1)
            root(0, 8, 0)
            normed(0)
            logits_evac(0)
            for n in range(2):
                act.wait_ge(x1_ready, 2 + n)
                squares(1, slice(n * BANK, (n + 1) * BANK), 9 if n else 1)
            act.wait_ge(sq_ready, 3)
            act.wait_ge(half_mean, 1)
            root(1, 9, 6)
            logits_evac(1)
            normed(1)
            for b in range(TB):
                act.wait_ge(top_ready, b + 1)
                last = act.activation(stat(72 + 4 * b, 4), stat(80 + 8 * b, 4), ACT.Exp, bias=stat(20 + b),
                                      accum_out=stat(22 + b))
                last.then_inc(gexp_ready, 1)
            def sigmoid_glu(n):
                act.wait_ge(glu_ready, n + 1)
                act.activation(sg, g_act, ACT.Sigmoid, scale=ALPHA).then_inc(sig_ready, 1)

            def evac_gu(n):
                act.wait_ge(gu_used, n * KD + KD)
                wait_pos(act, gut_done, n)
                act.activation(gu_sb[:, :], bank(0, 2), ACT.Copy).then_inc(gu_out, 1)

            def evac_sel(n):
                act.wait_ge(selt_done, n + 1)
                act.wait_ge(scat_done, 2 * n + 2)
                act.activation(sel[:, :], bank(4)[:, 0:T], ACT.Copy).then_inc(sel_ready, 1)

            def evac_y(n):
                act.wait_ge(dn_used, n * 4 + 4)
                wait_pos(act, scat_done, 2 * n + 2)
                act.activation(y_sb[:, :], bank(7), ACT.Copy).then_inc(y_ready, 1)

            def evac_gathered(n):
                act.wait_ge(gath_done, n + 1)
                wait_pos(act, xt_done, n)
                act.activation(spare[:, :], bank(6), ACT.Copy).then_inc(xn_ready, 1)

            def act_step(e):
                sigmoid_glu(e - 1)
                evac_gu(e)
                evac_gathered(e + 1)
                evac_sel(e - 1)
                evac_y(e - 1)

            act.wait_ge(gates_ready, 1)
            evac_gathered(0)
            act.wait_ge(gates_turned, 1)
            act.activation(gate_rows, bank(5)[0:E, 0:T], ACT.Copy).then_inc(gate_rows_ready, 1)
            evac_gu(0)
            act.wait_ge(lists_ready, 1)
            evac_gathered(1)
            act_step(1)
            with act.Fori(2, E - 1) as e:
                act_step(e)
            sigmoid_glu(E - 2)
            evac_gu(E - 1)
            evac_sel(E - 2)
            evac_y(E - 2)
            sigmoid_glu(E - 1)
            evac_y(E - 1)
            evac_sel(E - 1)

            def evac_ple_proj(i):
                act.wait_ge(pproj_done, i + 1)
                act.activation(pproj[:, i // 2, i % 2 * BANK:(i % 2 + 1) * BANK], bank(i), ACT.Copy).then_inc(pproj_out, 1)

            evac_ple_proj(0)

            act.wait_ge(lists_ready, 1)
            n_extra = act.value_load(lists[0:1, 2 * N_EXTRA:2 * N_EXTRA + 1], min_val=0, max_val=N_EXTRA)
            with act.If(n_extra > 0):
                with act.Fori(0, n_extra) as i:
                    n = i + E
                    evac_gathered(n)
                    evac_sel(n)
                    evac_gu(n)
                    sigmoid_glu(n)
                    evac_y(n)

            evac_ple_proj(1)
            evac_ple_proj(2)
            for b in range(TB):
                act.wait_ge(x2_ready, b + 1)
                squares(b, slice(0, D), 8 + b)
                if b == 0:
                    evac_ple_proj(3)
            for b in range(TB):
                act.wait_ge(sq_ready, 4 + b)
                root(b, 8 + b, 0)
            for b in range(TB):
                act.wait_ge(rstd_ready, 3 + b)
                for n in range(2):
                    act.wait_ge(gate_done, 2 * b + n + 1)
                    act.activation(gate_s[:, b, n * BANK:(n + 1) * BANK], bank(2 * b + n), ACT.Sigmoid,
                                   scale=stat(12 + b)).then_inc(gate_out, 1)
                act.activation(stat(60 + b), stat(0), ACT.Sqrt)
                for n in range(2):
                    act.wait_ge(x3_ready, 2 * b + n + 1)
                    act.activation(hfn[:, b, n * BANK:(n + 1) * BANK], acc[:, b, n * BANK:(n + 1) * BANK], ACT.Square,
                                   accum_out=stat(16 + 2 * b + n)).then_inc(fin_sq, 1)
                act.wait_ge(fin_sum, b + 1)
                act.activation(stat(72 + b), stat(74 + b), ACT.Sqrt, bias=stat(0), scale=1.0 / D).then_inc(fin_sqrt, 1)
                if b == 0:
                    act.activation(stat(62), stat(0), ACT.Sigmoid)
                act.wait_ge(fin_rstd, b + 1)
                act.activation(gate_s[:, b, BANK:D], gate_s[:, b, BANK:D], ACT.Copy,
                               scale=stat(76 + b)).then_inc(fin_ready, 1)

        @block.tensor
        def _(pe):
            def mm(o, l, r, start, stop, **kw):
                return pe.matmul(o, l, r, start=start, stop=stop, **kw)

            pe.wait_ge(consts_made, 2)
            for k in range(KD):
                pe.wait_ge(h_ready[k], 1)
                pe.wait_ge(s_qkvu[k], 16)
                w = ring[:, k, :]
                for j in range(12):
                    col = j * P if j < 8 else 3 * AW + (j - 8) * P
                    at = j if j < 8 else j + 4
                    last = mm(ps[:, at * T:(at + 1) * T], w[:, col:col + P], h_t[:, k, :], k == 0 and j % 2 == 0,
                              k == KD - 1, skip_group_check=True)
                last.then_inc(qkvu_used, 1)
                if k == 0:
                    pe.wait_ge(s_relb, 32)
                    mm(bank(5)[0:HEADS, 0:T], relb[:, :], onehot, True, True).then_inc(bias_mm, 1)
                if k == 1:
                    pe.wait_ge(squares_added, 1)
                    mm(bank(4)[:, 0:T], ones[:, :], x_ss, True, True).then_inc(sumsq_done, 1)
                if k == 3:
                    pe.wait_ge(row_ready, 1)
                    pe.wait_ge(bias_copied, 1)
                    for b in range(TB):
                        last = pe.transpose(bank(5)[:, b * P:(b + 1) * P], row256[:, b * P:(b + 1) * P], ident[:, :])
                    last.then_inc(row_turned, 1)
            pe.wait_ge(col_ready, 1)
            for k in range(KD):
                for b in range(TB):
                    last = mm(bank(4 + b), h_t[:, k, b * P:(b + 1) * P], ring[:, k, 2 * AW:3 * AW],
                              k == 0, k == KD - 1)
                last.then_inc(v_done, 1)

            def g_pair(i):
                if i >= 2:
                    pe.wait_ge(g_scaled, i - 1)
                for j in range(2):
                    for k in range(KD):
                        if i == 0:
                            pe.wait_ge(s_g[k], 16)
                        last = mm(bank(6 + i % 2)[:, j * T:(j + 1) * T],
                                  ring[:, (8 + k) % 12, (2 * i + j) * P:(2 * i + j + 1) * P], h_t[:, k, :],
                                  k == 0, k == KD - 1)
                last.then_inc(g_done, 1)

            pe.wait_ge(u_out, 2)
            g_pair(0)
            g_pair(1)
            pe.wait_ge(qkvu_out, 4)
            for c in range(4):
                for h in range(2):
                    hp, r = 4 * h + c, slice(h * DH, (h + 1) * DH)
                    last = mm(ps[:, hp * T:(hp + 1) * T], q_t[r, c, P:T], k_t[r, c, :], True, True)
            last.then_inc(scores_done, 1)
            pe.wait_ge(v_out, 2)
            for c in range(4):
                for h in range(2):
                    hp, r = 4 * h + c, slice(h * DH, (h + 1) * DH)
                    last = mm(ps[:, 4 * BANK + hp * P:4 * BANK + (hp + 1) * P], q_t[r, c, 0:P], k_t[r, c, 0:P],
                              True, True)
            last.then_inc(scores_done, 1)
            for i in range(2, 8):
                g_pair(i)
            pe.wait_ge(pooled_ready, 1)
            pe.wait_ge(s_pw, 16)
            for i in (8, 9):
                pe.wait_ge(g_scaled, i - 1)
                for j in range(2):
                    g = 2 * (i - 8) + j
                    last = mm(bank(6 + i % 2)[:, j * T:(j + 1) * T], pw_sb[:, g, :], pooled[:, g, :], True, True)
                last.then_inc(g_done, 1)
            pe.wait_ge(prob_ready, 2)
            for j in range(24):
                hp, s = divmod(j, 3)
                src = prob0[:, hp, :] if s == 2 else prob1[:, hp, s * P:(s + 1) * P]
                last = pe.transpose(ps[:, j * P:(j + 1) * P], src, ident[:, :])
                if j % 4 == 3:
                    last.then_inc(probt_done, 1)
            pe.wait_ge(g_out, 10)
            pe.wait_ge(probt_out, 6)
            for c in range(4):
                for b, kc in ((0, 0), (1, 0), (1, 1)):
                    for h in range(2):
                        hp = 4 * h + c
                        j = 3 * hp + (2 if b == 0 else kc)
                        last = mm(bank(6, 2)[h * DH:(h + 1) * DH, c * T + b * P:c * T + (b + 1) * P],
                                  v_n[:, kc, (2 * c + h) * DH:(2 * c + h + 1) * DH], prob_t[:, j, :],
                                  kc == 0, kc == b)
                if c % 2:
                    last.then_inc(pv_done, 1)
            for which, src, first, done in ((0, pool2_t, 0, po_done), (1, attn_t, 4, ao_done)):
                if which == 1:
                    pe.wait_ge(attn_out, 2)
                for jj in range(4):
                    for j in range(2):
                        col = (2 * jj + j) * P
                        for k in range(4):
                            if jj == 0 and j == 0 and k == 0:
                                pe.wait_ge(s_wo[which], 32)
                            last = mm(bank(first + jj)[:, j * T:(j + 1) * T],
                                      slot2(4 + 2 * which + k // 2)[:, k % 2, col:col + P], src[:, k, :],
                                      k == 0, k == 3)
                    last.then_inc(done, 1)
            rw = consts[:, C_RW:C_RW + KD * E].rearrange("p (c e) -> p c e", c=KD)

            def turn_x(b, chunks):
                for c in chunks:
                    last = pe.transpose(bank(4 + 2 * b, 2)[:, c * P:(c + 1) * P], acc[:, b, c * P:(c + 1) * P],
                                        ident[:, :])
                last.then_inc(turned, 1)

            def w_out_part(b, n, chunks):
                for k in chunks:
                    if b == 0 and n == 0:
                        pe.wait_ge(merged_ready, k // 2 + 1)
                        pe.wait_ge(s_wout[k // 4], 32)
                    last = mm(bank(2 * b + n), merged[:, k, b * P:(b + 1) * P],
                              slot2(8 + k // 2)[:, k % 2, n * BANK:(n + 1) * BANK], k == 0, k == KD - 1)
                    if (b, n) == (1, 1) and k % 2:
                        last.then_inc(wout_used, 1)
                if (b, n) != (1, 1) and k == KD - 1:
                    last.then_inc(wout_done, 1)

            def logits_t(b, chunks):
                for c in chunks:
                    q = c % 4
                    last = mm(bank(b)[E * q:E * (q + 1), 0:P], rw[:, c, :], hf_t[b][:, c, :], c < 4, c >= 4)
                if c == KD - 1:
                    last.then_inc(logits_mm, 1)

            def logits(b):
                pe.wait_ge(logits_out, b + 1)
                pe.transpose(bank(b)[:, P:2 * P], lt_sb[:, b, :], ident[:, :]).then_inc(logits_done, 1)

            w_out_part(0, 0, range(KD))
            w_out_part(0, 1, range(KD))
            w_out_part(1, 0, range(0, 2))
            pe.wait_ge(x1_ready, 1)
            pe.wait_ge(merged_ready, 4)
            turn_x(0, range(KD))
            w_out_part(1, 0, range(2, 5))
            pe.wait_ge(s_pack, 16)
            pe.wait_ge(turned_out, 1)
            logits_t(0, range(KD))
            w_out_part(1, 0, range(5, KD))
            logits(0)
            w_out_part(1, 1, range(0, 4))
            pe.wait_ge(x1_ready, 2)
            turn_x(1, range(0, 4))
            w_out_part(1, 1, range(4, 6))
            pe.wait_ge(chosen_ready, 1)
            mm(bank(2)[:, 0:E], tri[:, :], chosen[:, 0, :], True, True)
            mm(bank(2)[:, E:2 * E], ones[:, :], chosen[:, 0, :], True, False)
            w_out_part(1, 1, range(6, KD))
            pe.wait_ge(x1_ready, 3)
            turn_x(1, range(4, KD))
            for half in range(2):
                pe.wait_ge(turned_out, 2 + half)
                logits_t(1, range(4 * half, 4 * half + 4))
            logits(1)
            pe.wait_ge(chosen_ready, 2)
            mm(bank(2)[:, E:2 * E], tri[:, :], chosen[:, 1, :], False, True).then_inc(rank_done, 1)

            def gather(n, h, scattered):
                pe.wait_ge(pick_ready, n + 1)
                wait_pos(pe, added, 2 * scattered)
                wait_pos(pe, xg_ready, n)
                for b in range(TB):
                    for half in range(2):
                        last = mm(bank(6)[SLOTS * half:SLOTS * (half + 1), :], pick[:, h, b, :],
                                  hfn[:, b, half * BANK:(half + 1) * BANK], b == 0, b == TB - 1)
                last.then_inc(gath_done, 1)

            def turn_gathered(n):
                pe.wait_ge(xn_ready, n + 1)
                for c in range(4):
                    last = pe.transpose(bank(6)[:, c * P:(c + 1) * P], spare[:, c * P:(c + 1) * P], ident[:, :])
                last.then_inc(xt_done, 1)

            def turn_sel(n, scattered):
                pe.wait_ge(pickg_ready, n + 1)
                pe.wait_ge(added, 2 * scattered)
                for b in range(TB):
                    last = pe.transpose(bank(4)[:, b * P:(b + 1) * P],
                                        pick_g[:, b, :, :].rearrange("p a s -> p (a s)"), ident[:, :])
                last.then_inc(selt_done, 1)

            def gate_up(n, h, landed):
                pe.wait_ge(xg_ready, n + 1)
                wait_pos(pe, gu_out, n)
                for k in range(KD):
                    pe.wait_ge(s_gu[h][k], landed)
                    for q in range(4):
                        half = slice(SLOTS * (q % 2), SLOTS * (q % 2 + 1))
                        last = mm(bank(q // 2)[half, :], xg[:, h, k, :], ring[:, 8 * h + k, q * BANK:(q + 1) * BANK],
                                  k == 0, k == KD - 1)
                    last.then_inc(gu_used, 1)

            def down(n, scattered, landed, first=16, arrivals=s_dn):
                pe.wait_ge(hid_ready, n + 1)
                wait_pos(pe, added, 2 * scattered)
                hid4 = hid.rearrange("p (b q a s) -> p b q a s", b=2, q=2, a=2)
                for u in range(4):
                    pe.wait_ge(arrivals[u], landed)
                    for j in range(2):
                        k = 2 * u + j
                        for half in range(2):
                            last = mm(bank(7)[SLOTS * half:SLOTS * (half + 1), :], hid4[:, k // 4, k % 2, k // 2 % 2, :],
                                      slot2(first + u)[:, j, half * BANK:(half + 1) * BANK], k == 0, k == KD - 1)
                    last.then_inc(dn_used, 1)

            def turn_gu(n):
                pe.wait_ge(gu_out, n + 1)
                wait_pos(pe, gut_read, n)
                pairs = gu_sb[:, :].rearrange("p (t r k) -> p t r k", t=4, k=2)
                for kind in range(2):
                    for t in range(4):
                        last = pe.transpose(bank(2 + kind)[:, t * P:(t + 1) * P], pairs[:, t, :, kind], ident[:, :])
                last.then_inc(gut_done, 1)

            def scatter(n, scattered, gathered):
                pe.wait_ge(y_ready, n + 1)
                pe.wait_ge(sel_ready, n + 1)
                pe.wait_ge(added, 2 * scattered)
                for b in range(TB):
                    if b == 1:
                        pe.wait_ge(xg_ready, gathered)
                    for half in range(2):
                        r = slice(SLOTS * half, SLOTS * (half + 1))
                        last = mm(bank(4 + 2 * b + half), sel[r, b * P:(b + 1) * P], y_sb[r, :], True, True)
                    last.then_inc(scat_done, 1)

            pe.wait_ge(norm_ready, 2)
            gather(0, 0, 0)
            mm(bank(3)[0:1, 0:E], ones[:, 0:1], chosen[:, 0, :], True, False)
            mm(bank(3)[0:1, 0:E], ones[:, 0:1], chosen[:, 1, :], False, True).then_inc(count_done, 1)
            pe.wait_ge(gates_ready, 1)
            for b in range(TB):
                last = pe.transpose(bank(5)[0:E, b * P:(b + 1) * P], gates[:, b, :], ident[:, :])
            last.then_inc(gates_turned, 1)
            turn_gathered(0)
            gate_up(0, 0, 16)
            gather(1, 1, 0)
            pe.wait_ge(counts_read, 1)
            turn_gu(0)
            turn_gathered(1)
            pe.wait_ge(gate_rows_ready, 1)
            pe.wait_ge(s_bd, 32)
            pe.wait_ge(xg_ready, 2)
            for b in range(TB):
                for half in range(2):
                    last = mm(bank(4 + 2 * b + half), gate_rows[:, b * P:(b + 1) * P], bd_half[half], True, True)
                last.then_inc(scat_done, 1)

            def pe_step(e, h, gu_landed):
                gate_up(e, h, gu_landed)
                gather(e + 1, 1 - h, e)
                turn_sel(e - 1, e)
                down(e - 1, e, e * 16)
                turn_gathered(e + 1)
                turn_gu(e)
                scatter(e - 1, e, e + 2)

            pe_step(1, 1, 16)
            with pe.Fori(1, E // 2 - 1) as it:
                for h in range(2):
                    pe_step(2 * it + h, h, it * 16 + 16)
            pe_step(E - 2, 0, 8 * E)
            gate_up(E - 1, 1, 8 * E)
            turn_sel(E - 2, E - 1)
            down(E - 2, E - 1, 16 * (E - 1))
            turn_gu(E - 1)
            scatter(E - 2, E - 1, E)
            down(E - 1, E, 16, 0, s_dn_last)
            turn_sel(E - 1, E)

            def ple_proj(b, n):
                for k in range(2):
                    last = mm(bank(2 * b + n), pt_sb[:, k, b * P:(b + 1) * P], wpp[:, k, n * BANK:(n + 1) * BANK],
                              k == 0, k == 1)
                last.then_inc(pproj_done, 1)

            pe.wait_ge(s_ple_proj, 32)
            ple_proj(0, 0)
            scatter(E - 1, E, E)

            pe.wait_ge(lists_ready, 1)
            n_extra = pe.value_load(lists[0:1, 2 * N_EXTRA:2 * N_EXTRA + 1], min_val=0, max_val=N_EXTRA)
            with pe.If(n_extra > 0):
                with pe.Fori(0, n_extra) as i:
                    n = i + E
                    gather(n, 1, n + 1)
                    turn_sel(n, n + 1)
                    turn_gathered(n)
                    pe.wait_ge(pproj_out, 1)
                    gate_up(n, 1, i * 16 + (E // 2 + 1) * 16)
                    turn_gu(n)
                    down(n, n + 1, i * 16 + 32, 0, s_dn_last)
                    scatter(n, n + 1, n + 1)

            ple_proj(0, 1)
            ple_proj(1, 0)
            pe.wait_ge(x2_ready, 1)
            turn_x(0, range(KD))
            ple_proj(1, 1)
            for b in range(TB):
                pe.wait_ge(turned_out, 4 + b)
                for n in range(2):
                    pe.wait_ge(pproj_out, 2 * b + n + 1)
                    for k in range(KD):
                        pe.wait_ge(s_dn[k // 2], 16 * E)
                        last = mm(bank(2 * b + n), hp_t[:, k, b, :], wpg[:, k, n * BANK:(n + 1) * BANK],
                                  k == 0, k == KD - 1)
                    last.then_inc(gate_done, 1)
                    if b == 0 and n == 0:
                        pe.wait_ge(x2_ready, 2)
                        turn_x(1, range(KD))

        @block.vector
        def _(dve):
            chain = Chain(dve, dve_chain)
            tt, ts, stt = dve.tensor_tensor, dve.tensor_scalar, dve.scalar_tensor_tensor
            dve.memset(stat(0), EPS).then_inc(eps_ready, 1)
            dve.wait_ge(s_norms, 16)
            for c in range(1, KD, 2):
                dve.wait_ge(s_xt[c // 4], 16)
                ts(h_t[:, c, :], x_raw[:, c, :], consts[:, C_MIX + c:C_MIX + c + 1], None,
                   ALU.mult).then_inc(h_ready[c], 1)
            for c in range(1, KD, 2):
                tt(x_sq[:, c, :], x_raw[:, c, :], x_raw[:, c, :], ALU.mult).then_inc(squared, 1)
            dve.wait_ge(squared, KD)
            dve.tensor_reduce(x_ss, x_sq.rearrange("p c t -> p t c"), AX, ALU.add).then_inc(squares_added, 1)
            dve.wait_ge(rms_sqrt, 1)
            dve.reciprocal(row256[:, :], row256[:, :]).then_inc(row_ready, 1)
            dve.wait_ge(cnt_ready, 1)
            dve.reciprocal(gu_sb[:, :], gu_sb[:, :]).then_inc(inv_ready, 1)
            dve.wait_ge(row_turned, 1)
            dve.tensor_copy(stat(2, 2), bank(5)[:, 0:T:P]).then_inc(col_ready, 1)
            rstd2 = row256[:, :].unsqueeze(1).to_broadcast([P, 2, T])

            def times_rstd(out, b):
                return tt(out, bank(b).rearrange("p (c t) -> p c t", c=2), rstd2, ALU.mult)

            dve.wait_ge(row_ready, 1)
            dve.wait_ge(qkvu_used, KD)
            for j in range(2):
                times_rstd(u_t[:, 2 * j:2 * j + 2, :], 6 + j).then_inc(u_out, 1)
            for j in range(2):
                times_rstd(q_t[:, 2 * j:2 * j + 2, :], j).then_inc(qkvu_out, 1)
                times_rstd(k_t[:, 2 * j:2 * j + 2, :], 2 + j).then_inc(qkvu_out, 1)

            def scale_g(i):
                dve.wait_ge(g_done, i + 1)
                times_rstd(g_t[:, 2 * i:2 * i + 2, :], 6 + i % 2).then_inc(g_scaled, 1)

            scale_g(0)
            scale_g(1)
            dve.wait_ge(s_bias_in, 32)
            for i, (prob, src, bs) in enumerate(((prob1, ps[:, 0:4 * BANK], bias),
                                                 (prob0, ps[:, 4 * BANK:6 * BANK], bias[:, :, P:T]))):
                dve.wait_ge(scores_done, i + 1)
                chain(stt(out=prob, in0=src.rearrange("p (h k) -> p h k", h=HEADS), scalar=DH ** -0.5, in1=bs,
                          op0=ALU.mult, op1=ALU.add))
                chain(dve.tensor_reduce(stat(24 + 8 * i, 8), prob, AX, ALU.max))
                ts(stat(40 + 8 * i, 8), stat(24 + 8 * i, 8), -1.0, None, ALU.mult).then_inc(max_ready, 1)
            for i, prob in enumerate((prob1, prob0)):
                scale_g(2 + i)
                dve.wait_ge(exp_done, 8 + 8 * i)
                chain(dve.reciprocal(stat(24 + 8 * i, 8), stat(56 + 8 * i, 8)))
                tt(prob, prob, stat(24 + 8 * i, 8).unsqueeze(2).to_broadcast([P, HEADS, prob.shape[2]]),
                   ALU.mult).then_inc(prob_ready, 1)
            for i in range(4, 8):
                scale_g(i)
            for i in range(1, 6, 2):
                dve.wait_ge(probt_done, i + 1)
                dve.tensor_copy(prob_t[:, 4 * i:4 * i + 4, :].rearrange("p j q -> p (j q)"),
                                bank(i)).then_inc(probt_out, 1)
            dve.wait_ge(pv_done, 2)
            dve.tensor_copy(attn_t[:, 2:4, :].rearrange("p c t -> p (c t)"), bank(7)).then_inc(attn_out, 1)
            dve.wait_ge(g_out, 10)
            for jj in range(4):
                dve.wait_ge(po_done, jj + 1)
                m = mid[:, jj * BANK:(jj + 1) * BANK]
                chain(tt(m, bank(jj), g_t[:, 8 + 2 * jj:10 + 2 * jj, :].rearrange("p c t -> p (c t)"), ALU.mult))
            for jj in range(4):
                dve.wait_ge(ao_done, jj + 1)
                m = mid[:, jj * BANK:(jj + 1) * BANK]
                chain(tt(branch, bank(4 + jj), g_t[:, 2 * jj:2 * jj + 2, :].rearrange("p c t -> p (c t)"),
                         ALU.mult))
                ins = tt(m, m, branch, ALU.add)
                ins.then_inc(merged_ready, 1)
                dve.wait_ge(merged_ready, jj + 1)
            dve.wait_ge(s_x, 16)

            def turned_evac(n, b, col, view, first=0, chunks=KD):
                dve.wait_ge(turned, n + 1)
                tt(view[:, first:first + chunks, :],
                   bank(4 + 2 * b, 2).rearrange("p (c t) -> p c t", c=KD)[:, first:first + chunks, :],
                   consts[:, col + first:col + first + chunks].unsqueeze(2).to_broadcast([P, chunks, P]),
                   ALU.mult).then_inc(turned_out, 1)

            def make_rstd(n, b):
                dve.wait_ge(sqrt_ready, n + 1)
                dve.reciprocal(stat(12 + b), stat(10 + b)).then_inc(rstd_ready, 1)
                dve.wait_ge(rstd_ready, n + 1)

            idx = hot_g[:, 0, 0:16].bitcast(U32)
            idx1 = hot_g[:, 1, 0:8]
            logits = rank1

            def choose(b):
                dve.wait_ge(logits_done, b + 1)
                chain(dve.tensor_reduce(logits[:, b, :], bank(b)[:, P:2 * P].rearrange("p (q e) -> p e q", q=4), AX,
                                        ALU.add))
                chain(stt(out=logits[:, b, :], in0=logits[:, b, :], scalar=stat(12 + b), in1=rb_bc[:, :],
                          op0=ALU.mult, op1=ALU.add))
                chain(dve.max(stat(80 + 8 * b, 8), logits[:, b, :]))
                chain(dve.max_index(idx[:, 8 * b:8 * b + 8], stat(80 + 8 * b, 8), logits[:, b, :]))
                chain(ts(idx1[:, 4 * b:4 * b + 4], idx[:, 8 * b:8 * b + 4], 1.0, None, ALU.add))
                chain(tt(hot[:, 4 * b:4 * b + 4, :], iota1[:, 0:E].unsqueeze(1).to_broadcast([P, TOP_K, E]),
                         idx1[:, 4 * b:4 * b + 4].unsqueeze(2).to_broadcast([P, TOP_K, E]), ALU.is_equal))
                dve.tensor_reduce(chosen[:, b, :], hot[:, TOP_K * b:TOP_K * (b + 1), :]
                                  .rearrange("p k e -> p e k"), AX, ALU.add).then_inc(chosen_ready, 1)
                ts(stat(20 + b), stat(80 + 8 * b), -1.0, None, ALU.mult).then_inc(top_ready, 1)

            dve.wait_ge(wout_done, 2)
            tt(acc[:, 0, :], acc[:, 0, :], bank(0, 2), ALU.add).then_inc(x1_ready, 1)
            dve.wait_ge(s_pack, 16)
            turned_evac(0, 0, C_FFN, hf_t[0])
            make_rstd(0, 0)
            dve.wait_ge(wout_done, 3)
            tt(acc[:, 1, 0:BANK], acc[:, 1, 0:BANK], bank(2), ALU.add).then_inc(x1_ready, 1)
            dve.wait_ge(s_rb, 16)
            choose(0)
            turned_evac(1, 1, C_FFN, hf_t[1], 0, 4)
            dve.wait_ge(sq_ready, 2)
            ts(stat(6), stat(1), 1.0 / D, EPS, ALU.mult, ALU.add).then_inc(half_mean, 1)
            dve.wait_ge(wout_used, 4)
            tt(acc[:, 1, BANK:D], acc[:, 1, BANK:D], bank(3), ALU.add).then_inc(x1_ready, 1)
            turned_evac(2, 1, C_FFN, hf_t[1], 4, 4)
            make_rstd(1, 1)
            choose(1)
            dve.wait_ge(chosen_ready, 2)
            dve.wait_ge(rank_done, 1)
            chain(stt(out=rank1[:, :, :], in0=bank(2)[:, 0:TB * E].rearrange("p (b e) -> p b e", b=TB), scalar=1.0,
                      in1=chosen[:, :, :], op0=ALU.add, op1=ALU.mult))

            def column(table, e):
                one = table[:, :, e:e + 1] if isinstance(e, int) else table[:, :, bass.ds(e, 1)]
                return one.to_broadcast([P, TB, SLOTS])

            def make_pick(n, h, e, gathered, first=0):
                wait_pos(dve, gath_done, gathered)
                slots = iota1[:, 0:SLOTS] if isinstance(first, int) else iota1[:, bass.ds(first, SLOTS)]
                tt(pick[:, h, :, :], slots.unsqueeze(1).to_broadcast([P, TB, SLOTS]), column(rank1, e),
                   ALU.is_equal).then_inc(pick_ready, 1)

            def make_pick_g(n, h, e):
                wait_pos(dve, selt_done, n)
                dve.wait_ge(pick_ready, n + 1)
                for a in range(2):
                    ins = tt(pick_g[:, :, a, :], pick[:, h, :, :], column(gates, e), ALU.mult)
                ins.then_inc(pickg_ready, 1)

            def xg_evac(n, h, served):
                dve.wait_ge(xt_done, n + 1)
                wait_pos(dve, gu_used, served * KD)
                tt(xg[:, h, :, :].rearrange("p (a c) s -> p a c s", a=2),
                   bank(6).rearrange("p (c a s) -> p a c s", c=4, a=2),
                   consts[:, C_FFN:C_FFN + KD].rearrange("p (a c) -> p a c", a=2).unsqueeze(3)
                   .to_broadcast([P, 2, 4, SLOTS]), ALU.mult).then_inc(xg_ready, 1)

            bgu = consts[:, C_BGU:C_BGU + 16 * E].rearrange("p (e k t) -> p e k t", e=E, k=2)

            def expert_bias(e, kind):
                one = bgu[:, e, kind, :] if isinstance(e, int) else \
                    bgu[:, bass.ds(e, 1), kind, :].rearrange("p o t -> p (o t)")
                return one.unsqueeze(2).to_broadcast([P, 8, SLOTS])

            def swiglu(n, e):
                def tiles(x):
                    return x.rearrange("p (t s) -> p t s", s=SLOTS)
                dve.wait_ge(gut_done, n + 1)
                chain(tt(tiles(g_act), tiles(bank(2)), expert_bias(e, 0), ALU.add))
                ts(g_act, g_act, LIMIT, None, ALU.min).then_inc(glu_ready, 1)
                tt(tiles(l_act), tiles(bank(3)), expert_bias(e, 1), ALU.add).then_inc(gut_read, 1)
                dve.wait_ge(gut_read, n + 1)
                chain(ts(l_act, l_act, LIMIT, -LIMIT, ALU.min, ALU.max))
                dve.wait_ge(glu_ready, n + 1)
                chain(stt(out=l_act, in0=l_act, scalar=1.0, in1=g_act, op0=ALU.add, op1=ALU.mult))
                dve.wait_ge(sig_ready, n + 1)
                wait_pos(dve, dn_used, n * 4)
                dve.wait_ge(scat_done, 2)
                tt(hid, l_act, sg, ALU.mult).then_inc(hid_ready, 1)

            def add_back(j):
                for b in range(TB):
                    dve.wait_ge(scat_done, 2 * j + b + 1)
                    tt(acc[:, b, :], acc[:, b, :], bank(4 + 2 * b, 2), ALU.add).then_inc(added, 1)

            make_pick(0, 0, 0, 0)
            dve.wait_ge(gexp_ready, 2)
            chain(dve.reciprocal(stat(22, 2), stat(22, 2)))
            chain(tt(stat(72, 8).rearrange("p (b k) -> p b k", b=TB), stat(72, 8).rearrange("p (b k) -> p b k", b=TB),
                     stat(22, 2).unsqueeze(2).to_broadcast([P, TB, TOP_K]), ALU.mult))
            chain(tt(hot_g[:, :, :], hot[:, :, :], stat(72, 8).unsqueeze(2).to_broadcast([P, TB * TOP_K, E]), ALU.mult))
            for b in range(TB):
                ins = dve.tensor_reduce(gates[:, b, :], hot_g[:, TOP_K * b:TOP_K * (b + 1), :]
                                        .rearrange("p k e -> p e k"), AX, ALU.add)
            ins.then_inc(gates_ready, 1)
            dve.wait_ge(gates_ready, 1)
            xg_evac(0, 0, 0)
            make_pick_g(0, 0, 0)
            dve.wait_ge(count_done, 1)
            has, place = spare[0:1, 0:3 * E], spare[0:1, 3 * E:6 * E]
            picked = spare[0:1, 6 * E:9 * E].rearrange("p (b e) -> p b e", b=3)
            place3 = place.rearrange("p (b e) -> p b e", b=3)
            sums = small[0:1, 24:24 + 2 * N_EXTRA + 1]
            for b in range(3):
                ins = ts(has[:, b * E:(b + 1) * E], bank(3)[0:1, 0:E], float(SLOTS * (b + 1)), None, ALU.is_gt)
            ins.then_inc(counts_read, 1)
            dve.wait_ge(counts_read, 1)
            chain(dve.tensor_tensor_scan(place, ones[0:1, 0:3 * E], has, 0.0, ALU.mult, ALU.add))
            chain(tt(place, place, has, ALU.mult))
            experts = iota1[0:1, 0:E].unsqueeze(1).to_broadcast([1, 3, E])
            blocks = iota1[0:1, 0:3].unsqueeze(2).to_broadcast([1, 3, E])
            for i in range(N_EXTRA):
                for j, code in enumerate((experts, blocks)):
                    chain(stt(out=picked, in0=place3, scalar=float(i + 1), in1=code, op0=ALU.is_equal,
                              op1=ALU.mult, accum_out=sums[:, j * N_EXTRA + i:j * N_EXTRA + i + 1]))
            chain(dve.tensor_reduce(sums[:, 2 * N_EXTRA:], has, AX, ALU.add))
            chain(ts(sums[:, 0:N_EXTRA], sums[:, 0:N_EXTRA], -1.0, 0.0, ALU.add, ALU.max))
            chain(ts(sums[:, N_EXTRA:2 * N_EXTRA], sums[:, N_EXTRA:2 * N_EXTRA], float(SLOTS), None, ALU.mult))
            dve.tensor_copy(lists[:, :], sums).then_inc(lists_ready, 1)

            make_pick(1, 1, 1, 0)
            xg_evac(1, 1, 0)

            def dve_step(e, h):
                swiglu(e - 1, e - 1)
                add_back(e - 1)
                make_pick(e + 1, 1 - h, e + 1, e)
                xg_evac(e + 1, 1 - h, e)
                make_pick_g(e, h, e)

            dve_step(1, 1)
            steps = 3
            start = chain.n
            with dve.Fori(1, E // 2 - 1) as it:
                for h in range(2):
                    chain.n = (it - 1) * (2 * steps) + (start + h * steps)
                    dve_step(2 * it + h, h)
            chain.n = start + steps * (E - 4)
            dve_step(E - 2, 0)
            swiglu(E - 2, E - 2)
            add_back(E - 2)
            make_pick_g(E - 1, 1, E - 1)
            swiglu(E - 1, E - 1)
            add_back(E - 1)
            add_back(E)
            dve.wait_ge(added, 2 * E + 2)
            start = chain.n

            n_extra = dve.value_load(lists[0:1, 2 * N_EXTRA:2 * N_EXTRA + 1], min_val=0, max_val=N_EXTRA)
            with dve.If(n_extra > 0):
                with dve.Fori(0, n_extra) as i:
                    n = i + E
                    e = dve.value_load(lists[0:1, bass.ds(i, 1)], min_val=0, max_val=E - 1)
                    first = dve.value_load(lists[0:1, bass.ds(i + N_EXTRA, 1)], min_val=0, max_val=T - SLOTS)
                    chain.n = i * steps + start
                    make_pick(n, 1, e, n, first)
                    make_pick_g(n, 1, e)
                    xg_evac(n, 1, n)
                    swiglu(n, e)
                    add_back(n + 1)
                    dve.wait_ge(added, 2 * n + 4)
            chain = Chain(dve, dve_tail_chain)

            for b in range(TB):
                dve.memset(stat(4 + b), 0.0).then_inc(x2_ready, 1)
            for b in range(TB):
                turned_evac(3 + b, b, C_PLE, hp_t[:, :, b, :])
                make_rstd(2 + b, b)
            dve.wait_ge(s_fg, 16)
            for b in range(TB):
                for n in range(2):
                    cols = slice(n * BANK, (n + 1) * BANK)
                    dve.wait_ge(gate_out, 2 * b + n + 1)
                    dve.wait_ge(pproj_out, 2 * b + n + 1)
                    chain(tt(gate_s[:, b, cols], gate_s[:, b, cols], pproj[:, b, cols], ALU.mult))
                    tt(acc[:, b, cols], acc[:, b, cols], gate_s[:, b, cols], ALU.add).then_inc(x3_ready, 1)
                    dve.wait_ge(x3_ready, 2 * b + n + 1)
                    chain(tt(gate_s[:, b, cols], acc[:, b, cols], fg_bc[:, cols], ALU.mult))
                dve.wait_ge(fin_sq, 2 * b + 2)
                tt(stat(74 + b), stat(16 + 2 * b), stat(17 + 2 * b), ALU.add).then_inc(fin_sum, 1)
                dve.wait_ge(fin_sqrt, b + 1)
                dve.reciprocal(stat(76 + b), stat(72 + b)).then_inc(fin_rstd, 1)
                dve.wait_ge(fin_rstd, b + 1)
                ts(gate_s[:, b, 0:BANK], gate_s[:, b, 0:BANK], stat(76 + b), None, ALU.mult).then_inc(fin_ready, 1)


def kernel(**inputs):
    from concourse import bacc
    from concourse.bass_utils import run_bass_kernel_spmd

    def f(name, *shape):
        return np.ascontiguousarray(inputs[name]).reshape(shape)

    columns = [f(n, -1, P).T for n in ("norm_mix_g", "norm_ffn_g", "norm_ple_g", "pool_scale")]
    router = f("router_w", KD, P, E).transpose(1, 0, 2).reshape(P, KD * E)
    bgu = f("b_gate_up", E, 2, 2, 2, P, 2).transpose(4, 0, 5, 1, 3, 2).reshape(P, E * 16)
    dist = T - 1 - np.arange(T)
    exact = BUCKETS // 2
    large = exact + (np.log(np.maximum(dist, 1) / exact) / math.log(MAX_DISTANCE / exact) * exact).astype(int)
    bucket = np.where(dist < exact, dist, np.minimum(large, BUCKETS - 1))
    arrays = {
        "x": f("x", T, D), "x_t": np.ascontiguousarray(f("x", T, D).T),
        "p_t": np.ascontiguousarray(f("p", T, PLE).T),
        "pack": np.ascontiguousarray(np.concatenate(columns + [router, bgu], axis=1)),
        "rel_bias": f("rel_bias", BUCKETS, HEADS),
        "bucket_of": (np.arange(BUCKETS)[:, None] == bucket[None, :]).astype(np.float32),
        "w_in": f("w_in", D, 2 * NW), "pool_w": f("pool_w", GROUPS, P, P),
        "w_o_attn": f("w_o_attn", AW, D), "w_o_pool": f("w_o_pool", AW, D), "w_out": f("w_out", D, D),
        "router_b": f("router_b", E), "w_gate_up": f("w_gate_up", E, D, NW), "w_down": f("w_down", E, D, D),
        "b_down": f("b_down", E, D), "w_ple_gate": f("w_ple_gate", D, D), "w_ple_proj": f("w_ple_proj", PLE, D),
        "norm_final_g": f("norm_final_g", D),
    }
    nc = bacc.Bacc("TRN2", target_bir_lowering=False, num_devices=1)
    args = {n: nc.dram_tensor(f"in_{n}", a.shape, mybir.dt.from_np(a.dtype), kind="ExternalInput").ap()
            for n, a in arrays.items()}
    out = nc.dram_tensor("out_0", (T, D), F32, kind="ExternalOutput").ap()
    block_kernel(nc, **args, out=out)
    r = run_bass_kernel_spmd(nc, [{f"in_{n}": a for n, a in arrays.items()}], core_ids=[0])
    return r.results[0]["out_0"].reshape(1, T, D)
```

```python
import math
from contextlib import ExitStack

import numpy as np

import concourse.bass as bass
from concourse import mybir

P = 128
D = 1024
T = 256
TB = T // P
KD = D // P
HEADS = 8
DH = 64
AW = HEADS * DH
NW = 2 * D
BUCKETS = 32
MAX_DISTANCE = 128
WINDOWS = (2, 4, 8, 16)
GROUPS = len(WINDOWS)
E = 32
TOP_K = 4
SLOTS = 64
N_EXTRA = 16
LIMIT = 7.0
ALPHA = 1.702
PLE = 256
EPS = 1e-6
NEG = -3.0e38
BANK = 512

BLOCK = NW // KD
BLOCKS = (0, 1, 2, 3, 6, 7, 4, 5) + tuple(range(8, 16))
N_IN = len(BLOCKS)
UNSPLIT = 2
RAW, HI = 4, 3
PLACES = [(u % RAW, RAW + u % HI) for u in range(N_IN)] + [(7, 11), (8, 5), (9, 6), (10, 0)] \
    + [(1, 12), (2, 11), (3, 7), (4, 8)]
U_O, U_OUT = N_IN, N_IN + 4
LO_ON_POOL = (U_O, U_O + 2, U_O + 3, U_OUT + 2, U_OUT + 3)
LO_ON_DVE = [u for u in range(UNSPLIT, U_OUT + 4) if u not in LO_ON_POOL]

C_MIX, C_FFN, C_PLE, C_POOL, C_RW, C_BGU = 0, 8, 16, 24, 28, 28 + KD * E
N_PACK = C_BGU + E * 16

ALU = mybir.AluOpType
ACT = mybir.ActivationFunctionType
AX = mybir.AxisListType.X
F32 = mybir.dt.float32
F32R = mybir.dt.float32r
I32 = mybir.dt.int32
U32 = mybir.dt.uint32


class Chain:

    def __init__(self, eng, sem):
        self.eng, self.sem, self.n = eng, sem, 0

    def __call__(self, ins):
        ins.then_inc(self.sem, 1)
        self.n = self.n + 1
        self.eng.wait_ge(self.sem, self.n)


def wait_pos(eng, sem, value):
    if not isinstance(value, int) or value > 0:
        eng.wait_ge(sem, value)


def block_kernel(nc, x, x_t, p_t, pack, rel_bias, bucket_of, w_in, pool_w, w_o_attn, w_o_pool, w_out,
                 router_b, w_gate_up, w_down, b_down, w_ple_gate, w_ple_proj, norm_final_g, out):
    ctx = ExitStack()
    with ctx:
        def sb(name, shape, dt=F32):
            return ctx.enter_context(nc.sbuf_tensor(name, shape, dt))

        def sem(name):
            return ctx.enter_context(nc.semaphore(name))

        bias_rows = nc.dram_tensor("bias_rows", (HEADS, P, 384), F32).ap()

        def sb_split(name, *shape):
            at = (nc.sbuf_base + 31) // 32 * 32
            return sb(name, [P, *shape]), [
                nc.alloc_sbuf_tensor_at(f"{name}_split{i}", [P, NW], F32R, offset=at + 4 * NW * i)
                for i in range(math.prod(shape) // NW)]

        ring, ring_split = sb_split("ring", 20, NW)
        acc, acc_split = sb_split("acc", TB, D)
        hfn, hfn_split = sb_split("hfn", TB, D)
        mid, mid_split = sb_split("mid", 2048)
        consts = sb("consts", [P, N_PACK])
        xg = sb("xg", [P, 2, KD, SLOTS])
        gu_sb = sb("gu_sb", [P, 2 * BANK])
        y_sb = sb("y_sb", [P, BANK])
        sel = sb("sel", [P, T])
        pick = sb("pick", [P, 2, TB, SLOTS])
        pick_g = sb("pick_g", [P, TB, 2, SLOTS])
        spare = sb("spare", [P, BANK])
        chosen = sb("chosen", [P, TB, E])
        gates = sb("gates", [P, TB, E])
        rank1 = sb("rank1", [P, TB, E])
        small = sb("small", [P, 96])
        iota1 = sb("iota1", [P, T])
        ident = sb("ident", [P, P])
        tri = sb("tri", [P, P])
        ones = sb("ones", [P, P])
        relb = sb("relb", [BUCKETS, HEADS])
        row256 = sb("row256", [P, T])
        rb_bc = sb("rb_bc", [P, E])
        lists = sb("lists", [1, 2 * N_EXTRA + 1], I32)

        hot = spare[:, 0:256].rearrange("p (k e) -> p k e", e=E)
        hot_g = spare[:, 256:512].rearrange("p (k e) -> p k e", e=E)

        h_t = ring[:, 12, :].rearrange("p (c t) -> p c t", c=KD)
        q_t = ring[:, 13, 0:1024].rearrange("p (c t) -> p c t", c=4)
        k_t = ring[:, 13, 1024:2048].rearrange("p (c t) -> p c t", c=4)
        v_n = ring[:, 14, 0:1024].rearrange("p (b n) -> p b n", b=TB)
        u_t = ring[:, 14, 1024:2048].rearrange("p (g t) -> p g t", g=GROUPS)
        g_t = ring[:, 15:17, :].rearrange("p s n -> p (s n)").rearrange("p (c t) -> p c t", t=T)
        bias = ring[:, 17, :].rearrange("p (h k) -> p h k", h=HEADS)
        h_hi = acc_split[0][:, :].rearrange("p (c t) -> p c t", c=KD)
        h_lo = mid_split[0][:, :].rearrange("p (c t) -> p c t", c=KD)
        pool2_hi, pool2_lo = (ring_split[17][:, i * 1024:(i + 1) * 1024]
                              .rearrange("p (g t) -> p g t", g=GROUPS) for i in range(2))
        prob1 = ring[:, 18, :].rearrange("p (h k) -> p h k", h=HEADS)
        prob0 = ring[:, 19, 0:1024].rearrange("p (h k) -> p h k", h=HEADS)
        attn_lo, attn_hi = (ring_split[18][:, i * 1024:(i + 1) * 1024]
                            .rearrange("p (c t) -> p c t", c=4) for i in range(2))
        prob_t = ring[:, 12:14, :].rearrange("p s n -> p (s n)")[:, 0:24 * P].rearrange("p (j q) -> p j q", q=P)
        x_raw = ring[:, 18, :].rearrange("p (c t) -> p c t", c=KD)
        x_sq = ring[:, 16, :].rearrange("p (c t) -> p c t", c=KD)
        x_ss = sel[:, :]
        win_a = hfn[:, 0, :].rearrange("p (g t) -> p g t", g=GROUPS)
        win_b = hfn[:, 1, :].rearrange("p (g t) -> p g t", g=GROUPS)
        inv_cnt = gu_sb[:, :].rearrange("p (g t) -> p g t", g=GROUPS)
        pooled = xg[:, :, :, :].rearrange("p a c s -> p (a c s)").rearrange("p (g t) -> p g t", g=GROUPS)
        branch = xg[:, 0, :, :].rearrange("p c s -> p (c s)")
        pw_sb = y_sb[:, :].rearrange("p (g d) -> p g d", g=GROUPS)
        onehot = spare[0:BUCKETS, 0:T]
        bias_v = xg[0:HEADS, :, :, :].rearrange("p a c s -> p (a c s)")[:, 0:384]
        merged_lo = mid_split[0][:, :].rearrange("p (c t) -> p c t", c=KD)
        merged_hi = hfn_split[0][:, :].rearrange("p (c t) -> p c t", c=KD)
        hf_t = [x[:, 0:KD * P].rearrange("p (c t) -> p c t", c=KD) for x in (gu_sb, ring[:, 18, :])]
        gate_rows = row256[0:E, :]
        lt_sb = pick[:, :, :, :].rearrange("p h b s -> p h (b s)")
        g_act, l_act, sg, hid = (mid[:, i * BANK:(i + 1) * BANK] for i in range(4))
        bd_half = (y_sb[0:E, :], hid[0:E, :])
        wpg = ring[:, 16:20, :].rearrange("p s (j n) -> p (s j) n", j=2)
        wpp = ring[:, 4, :].rearrange("p (j n) -> p j n", j=2)
        pt_sb = ring[:, 5, 0:512].rearrange("p (j t) -> p j t", j=2)
        fg_bc = ring[:, 5, 1024:2048]
        pproj = ring[:, 6, :].rearrange("p (b n) -> p b n", b=TB)
        gate_s = ring[:, 7, :].rearrange("p (b n) -> p b n", b=TB)
        hp_t = mid[:, :].rearrange("p (c b t) -> p c b t", c=KD, b=TB)

        def stat(a, n=1):
            return small[:, a:a + n]

        ps = ctx.enter_context(nc.psum_tensor("ps", [P, 8 * BANK], F32))

        def bank(b, n=1):
            return ps[:, b * BANK:(b + n) * BANK]

        s_xt = [sem(f"xt_landed{i}") for i in range(2)]
        s_norms, s_pack, s_pw, s_x, s_relb, s_rb, s_bd = (sem(n) for n in (
            "norms_landed", "pack_landed", "pool_w_landed", "x_landed", "rel_landed", "router_b_landed",
            "b_down_landed"))
        s_bias_out, s_bias_in = sem("bias_rows_stored"), sem("bias_landed")
        s_first = sem("first_half_unit_landed")
        s_win = [sem(f"w_in_landed{i}") for i in range(RAW)]
        s_wo = [sem(f"{n}_landed") for n in ("w_o_pool", "w_o_attn")]
        s_wout = [sem(f"wout_landed{i}") for i in range(2)]
        s_gu = [[sem(f"gu_landed{h}_{k}") for k in range(KD)] for h in range(2)]
        s_dn = [sem(f"down_landed{u}") for u in range(4)]
        s_dn_last = [sem(f"late_down_landed{u}") for u in range(4)]
        s_ple_proj, s_fg = sem("ple_proj_landed"), sem("final_g_landed")
        s_out = sem("out_stored")

        consts_made, eps_ready = sem("consts_made"), sem("eps_ready")
        dve_chain, dve_tail_chain, pool_chain = sem("dve_chain"), sem("dve_tail_chain"), sem("pool_chain")
        squared, squares_added = sem("squared"), sem("squares_added")
        sumsq_done = sem("sumsq_done")
        rms_sqrt, row_ready, row_turned, col_ready = (sem(n) for n in (
            "rms_sqrt", "rstd_row_ready", "rstd_row_turned", "rstd_column_ready"))
        h_ready = [sem(f"h_ready{i}") for i in range(2)]
        h_hi_ready, h_lo_ready = sem("h_hi_ready"), sem("h_lo_ready")
        unit_used, hi_ready, lo_ready = sem("w_in_unit_used"), sem("weight_hi_ready"), sem("weight_lo_ready")
        part_hi, pool_lo_ready = sem("merged_hi_ready"), sem("weight_lo_ready_from_pool")
        merged_full = sem("merged_full")
        v_out = sem("v_evacuated")
        bias_mm, bias_copied = sem("bias_mm"), sem("bias_copied")
        qk_out = sem("qk_evacuated")
        u_out = sem("u_evacuated")
        pooled_done, g_scaled, g_out = sem("pooled_done"), sem("g_scaled"), sem("mix_gates_ready")
        cnt_ready, inv_ready, pooled_ready = sem("cnt_ready"), sem("inv_ready"), sem("pooled_ready")
        scores_done, max_ready, exp_done, prob_ready = (sem(n) for n in (
            "scores_done", "max_ready", "exp_done", "prob_ready"))
        probt_done, probt_out = sem("prob_t_done"), sem("prob_t_evacuated")
        pv_done, attn_hi_out, attn_out = sem("pv_done"), sem("attn_hi_ready"), sem("attn_lo_ready")
        pool_hi_out, pool_lo_out = sem("pooled_hi_ready"), sem("pooled_lo_ready")
        ao_done, po_done, merged_ready = sem("attn_branch_done"), sem("pool_branch_done"), sem("merged_ready")
        wout_done, x1_ready = sem("wout_done"), sem("x1_ready")
        half_mean, x2_ready = sem("half_mean_ready"), sem("x2_ready")
        sq_ready, sqrt_ready, rstd_ready, norm_ready = (sem(n) for n in (
            "sumsq_ready", "sqrt_ready", "rstd_ready", "norm_ready"))
        turned, turned_out = sem("x_turned"), sem("x_turned_evacuated")
        logits_mm, logits_out = sem("logits_product"), sem("logits_evacuated")
        logits_done, top_ready, gexp_ready, chosen_ready, gates_ready = (sem(n) for n in (
            "logits_done", "top_ready", "gate_exp_ready", "chosen_ready", "gates_ready"))
        rank_done, rank_ready, count_done, gates_turned, gate_rows_ready = (sem(n) for n in (
            "rank_done", "rank_ready", "count_done", "gates_turned", "gate_rows_ready"))
        counts_read, lists_ready = sem("counts_read"), sem("lists_ready")
        pick_ready, gath_done, xg_ready = sem("pick_ready"), sem("gather_done"), sem("xg_ready")
        xn_ready, xt_done = sem("gathered_evacuated"), sem("gathered_turned")
        pickg_ready, selt_done, sel_ready = sem("pick_g_ready"), sem("sel_turned"), sem("sel_ready")
        gu_used, gu_out, gut_done, gut_read = (sem(n) for n in (
            "gu_used", "gu_evacuated", "gu_turned", "gu_turned_read"))
        glu_ready, sig_ready, hid_ready = sem("glu_ready"), sem("sigmoid_ready"), sem("hid_ready")
        dn_used, y_ready, scat_done, added = (sem(n) for n in ("down_used", "y_ready", "scatter_done", "added"))
        pproj_done, pproj_out = sem("ple_proj_done"), sem("ple_proj_evacuated")
        fin_sq, fin_sum, fin_sqrt, fin_rstd = (sem(n) for n in (
            "final_squares", "final_sum", "final_sqrt", "final_rstd"))
        gate_done, gate_out, x3_ready, fin_ready = (sem(n) for n in (
            "ple_gate_done", "ple_gate_sigmoid", "x3_ready", "final_ready"))

        block = ctx.enter_context(nc.Block())

        wo_units = [(w_o_pool, 0), (w_o_pool, 1), (w_o_attn, 0), (w_o_attn, 1)]

        def two_chunks(w, u):
            return w[2 * u * P:(2 * u + 2) * P, :].rearrange("(j p) n -> p j n", p=P)

        def slot2(s):
            return ring[:, s, :].rearrange("p (j n) -> p j n", j=2)

        def landed(eng, u):
            if u < U_O:
                eng.wait_ge(s_win[u % RAW], 16 * (u // RAW + 1))
            elif u < U_OUT:
                eng.wait_ge(s_wo[(u - U_O) // 2], 32)
            else:
                eng.wait_ge(s_wout[(u - U_OUT) // 2], 32)

        def split_in(u):
            return u - UNSPLIT + 1

        def wait_lo(eng, u):
            if u in LO_ON_POOL:
                eng.wait_ge(pool_lo_ready, LO_ON_POOL.index(u) + 1)
            else:
                eng.wait_ge(lo_ready, LO_ON_DVE.index(u) + 1)

        def hi_of(u):
            return ring_split[PLACES[u][1]][:, :]

        def lo_of(u):
            return ring_split[PLACES[u][0]][:, :]

        @block.sync
        def _(sp):
            def load_gu(e, h, k, landed):
                src = w_gate_up[e] if isinstance(e, int) else w_gate_up[bass.ds(e, 1)].rearrange("o d f -> (o d) f")
                sp.dma_start(ring[:, 8 * h + k, :], src[k * P:(k + 1) * P, :]).then_inc(landed, 16)

            def load_down(e, u, landed):
                src = w_down[e] if isinstance(e, int) else w_down[bass.ds(e, 1)].rearrange("o d f -> (o d) f")
                sp.dma_start(slot2(16 + u), two_chunks(src, u)).then_inc(landed, 16)

            half = BLOCK * KD // 2
            for i in range(2):
                sp.dma_start(x_raw[:, 4 * i:4 * i + 4, :], x_t[4 * i * P:4 * (i + 1) * P, :]
                             .rearrange("(c p) t -> p c t", p=P)).then_inc(s_xt[i], 16)
                sp.dma_start(ring[:, 0, i * half:(i + 1) * half], w_in[BLOCKS[0], :, i * half:(i + 1) * half]
                             ).then_inc(s_win[0] if i else s_first, 16)

            def load_in(u):
                if u >= RAW:
                    sp.wait_ge(unit_used, u - RAW + 1)
                sp.dma_start(ring[:, PLACES[u][0], :], w_in[BLOCKS[u]]).then_inc(s_win[u % RAW], 16)

            for u in range(1, RAW):
                load_in(u)
            sp.dma_start(consts[:, C_RW:], pack[:, C_RW:]).then_inc(s_pack, 16)
            sp.dma_start(pw_sb, pool_w.rearrange("g c d -> c g d")).then_inc(s_pw, 16)
            sp.dma_start(rb_bc[:, :], router_b.partition_broadcast(P)).then_inc(s_rb, 16)
            sp.wait_ge(bias_copied, 1)
            sp.dma_start(bias_rows[:, :, :], bias_v.unsqueeze(1).to_broadcast([HEADS, P, 384])).then_inc(s_bias_out, 16)
            load_in(4)
            load_in(5)
            sp.wait_ge(s_bias_out, 16)
            for par in range(2):
                src = bass.AP(tensor=bias_rows.tensor, offset=par * P * 384 + P - 1,
                              ap=[[384 - 1, P], [2 * P * 384, 4], [1, T]])
                sp.dma_start(bias[:, 4 * par:4 * par + 4, :], src).then_inc(s_bias_in, 16)
            for u in range(6, N_IN):
                load_in(u)
                if u >= N_IN - 4:
                    i = u - (N_IN - 4)
                    sp.dma_start(slot2(PLACES[U_O + i][0]), two_chunks(*wo_units[i])).then_inc(s_wo[i // 2], 16)
            for i in range(4):
                sp.wait_ge(unit_used, min(N_IN - 2 + i, N_IN))
                sp.dma_start(ring[:, PLACES[U_OUT + i][0], :], w_out[i]).then_inc(s_wout[i // 2], 16)
            sp.dma_start(acc[:, :, :], x.rearrange("(b p) d -> p b d", p=P)).then_inc(s_x, 16)
            sp.wait_ge(pv_done, 2)
            for k in (5, 6):
                load_gu(1, 1, k, s_gu[1][k])
            load_down(0, 3, s_dn[3])
            sp.wait_ge(po_done, 4)
            load_gu(0, 0, 5, s_gu[0][5])
            load_down(0, 1, s_dn[1])
            sp.wait_ge(ao_done, 4)
            for k in (0, 6):
                load_gu(0, 0, k, s_gu[0][k])
            for k in (1, 2):
                load_gu(1, 1, k, s_gu[1][k])
            sp.wait_ge(merged_full, 4)
            load_gu(1, 1, 7, s_gu[1][7])
            load_down(0, 0, s_dn[0])
            sp.wait_ge(wout_done, 2)
            for k in (1, 2):
                load_gu(0, 0, k, s_gu[0][k])
            for k in (3, 4):
                load_gu(1, 1, k, s_gu[1][k])
            sp.wait_ge(wout_done, 4)
            for k in (3, 4, 7):
                load_gu(0, 0, k, s_gu[0][k])
            load_gu(1, 1, 0, s_gu[1][0])

            sp.wait_ge(pooled_done, 2)
            sp.wait_ge(logits_mm, 2)
            load_down(0, 2, s_dn[2])
            for half in range(2):
                sp.dma_start(bd_half[half], b_down[:, half * BANK:(half + 1) * BANK]).then_inc(s_bd, 16)

            def next_gu(e, h, chunks=range(KD)):
                for k in chunks:
                    sp.wait_ge(gu_used, (e - 2) * KD + k + 1)
                    load_gu(e, h, k, s_gu[h][k])

            def next_down(e):
                for u in range(4):
                    sp.wait_ge(dn_used, (e - 1) * 4 + u + 1)
                    load_down(e, u, s_dn[u])

            GU_FIRST = 2

            def next_both(e, h):
                next_gu(e, h, range(GU_FIRST))
                next_down(e - 2)
                next_gu(e, h, range(GU_FIRST, KD))

            next_gu(2, 0)
            next_gu(3, 1)
            next_down(1)
            with sp.Fori(2, E // 2 - 1) as it:
                for h in range(2):
                    next_gu(2 * it + h, h)
                    next_down(2 * it + h - 2)
            for h in range(2):
                next_both(E - 2 + h, h)
            sp.wait_ge(gu_used, (E - 1) * KD)
            next_down(E - 2)
            sp.dma_start(pt_sb, p_t.rearrange("(j p) t -> p j t", p=P)).then_inc(s_ple_proj, 16)
            sp.dma_start(wpp, w_ple_proj.rearrange("(j p) n -> p j n", p=P)).then_inc(s_ple_proj, 16)
            for u in range(4):
                sp.dma_start(slot2(u), two_chunks(w_down[E - 1], u)).then_inc(s_dn_last[u], 16)
            for u in range(4):
                sp.wait_ge(dn_used, (E - 2) * 4 + u + 1)
                sp.dma_start(slot2(16 + u), two_chunks(w_ple_gate, u)).then_inc(s_dn[u], 16)
            sp.dma_start(fg_bc, norm_final_g.partition_broadcast(P)).then_inc(s_fg, 16)

            sp.wait_ge(lists_ready, 1)
            n_extra = sp.value_load(lists[0:1, 2 * N_EXTRA:2 * N_EXTRA + 1], min_val=0, max_val=N_EXTRA)
            with sp.If(n_extra > 0):
                with sp.Fori(0, n_extra) as i:
                    e = sp.value_load(lists[0:1, bass.ds(i, 1)], min_val=0, max_val=E - 1)
                    sp.wait_ge(gu_used, (i + E) * KD)
                    for k in range(KD):
                        load_gu(e, 1, k, s_gu[1][k])
                    sp.wait_ge(dn_used, (i + E) * 4)
                    for u in range(4):
                        src = w_down[bass.ds(e, 1)].rearrange("o d f -> (o d) f")
                        sp.dma_start(slot2(u), two_chunks(src, u)).then_inc(s_dn_last[u], 16)

            for b in range(TB):
                sp.wait_ge(fin_ready, 2 * b + 2)
                sp.dma_start(out[b * P:(b + 1) * P, :], gate_s[:, b, :]).then_inc(s_out, 16)
            sp.wait_ge(s_out, 32)

        @block.gpsimd
        def _(pool):
            chain = Chain(pool, pool_chain)
            pool.memset(ones[:, :], 1.0).then_inc(consts_made, 1)
            chain(pool.memset(ident[:, :], 0.0))
            chain(pool.affine_select(out=ident[:, :], in_=ident[:, :], compare_op=ALU.not_equal, fill=1.0,
                                     base=0, pattern=[[-1, P]], channel_multiplier=1))
            pool.wait_ge(consts_made, 1)
            chain(pool.affine_select(out=tri[:, :], in_=ones[:, :], compare_op=ALU.is_gt, fill=0.0,
                                     base=0, pattern=[[1, P]], channel_multiplier=-1))
            chain(pool.iota(iota1[:, :], pattern=[[1, T]], base=1, channel_multiplier=0,
                            allow_small_or_imprecise_dtypes=True))
            pool.memset(bias_v[:, 256:384], NEG).then_inc(consts_made, 1)
            for g, w in enumerate(WINDOWS):
                pool.memset(inv_cnt[:, g, w:], 1.0 / w)
                last = pool.tensor_scalar(inv_cnt[:, g, 0:w], iota1[:, 0:w], float(w), None, ALU.min)
            last.then_inc(cnt_ready, 1)

            pool.wait_ge(u_out, 2)
            pool.wait_ge(s_bias_out, 16)
            src = u_t
            for j in range(GROUPS):
                dst = (win_a, win_b)[j % 2]
                sh = 1 << j
                pool.tensor_copy(dst[:, j:, 0:sh], src[:, j:, 0:sh])
                chain(pool.tensor_tensor(dst[:, j:, sh:], src[:, j:, sh:], src[:, j:, 0:T - sh], ALU.add))
                if j == 0:
                    pool.wait_ge(inv_ready, 1)
                chain(pool.tensor_tensor(pooled[:, j, :], dst[:, j, :], inv_cnt[:, j, :], ALU.mult))
                last = pool.tensor_tensor(pooled[:, j, :], pooled[:, j, :], u_t[:, j, :], ALU.subtract)
                src = dst
            last.then_inc(pooled_ready, 1)
            for u in LO_ON_POOL:
                pool.wait_ge(hi_ready, split_in(u))
                pool.tensor_tensor(lo_of(u), ring[:, PLACES[u][0], :], hi_of(u).bitcast(F32),
                                   ALU.subtract).then_inc(pool_lo_ready, 1)

        @block.scalar
        def _(act):
            act.wait_ge(eps_ready, 1)
            act.activation(stat(63), stat(0), ACT.Sqrt)
            act.dma_start(consts[:, 0:C_RW], pack[:, 0:C_RW]).then_inc(s_norms, 16)
            act.dma_start(relb[:, :], rel_bias).then_inc(s_relb, 16)
            act.dma_start(onehot, bucket_of).then_inc(s_relb, 16)
            act.wait_ge(s_norms, 16)
            for c in range(0, KD, 2):
                act.wait_ge(s_xt[c // 4], 16)
                act.activation(h_t[:, c, :], x_raw[:, c, :], ACT.Copy,
                               scale=consts[:, C_MIX + c:C_MIX + c + 1]).then_inc(h_ready[0], 1)
            for c in range(0, KD, 2):
                act.activation(x_sq[:, c, :], x_raw[:, c, :], ACT.Square).then_inc(squared, 1)
            act.wait_ge(h_ready[0], KD // 2)
            act.wait_ge(h_ready[1], KD // 2)
            act.activation(h_hi, h_t, ACT.Copy).then_inc(h_hi_ready, 1)

            def hi(u):
                landed(act, u)
                if u < U_O:
                    wait_pos(act, unit_used, u - HI + 1)
                elif u < U_OUT:
                    wait_pos(act, unit_used, (0, 14, 15, 13)[u - U_O])
                elif u == U_OUT:
                    act.wait_ge(pv_done, 2)
                else:
                    act.wait_ge(po_done, 4)
                act.activation(hi_of(u), ring[:, PLACES[u][0], :], ACT.Copy).then_inc(hi_ready, 1)

            act.wait_ge(sumsq_done, 1)
            act.wait_ge(eps_ready, 1)
            act.activation(row256[:, :], bank(4)[:, 0:T], ACT.Sqrt, bias=stat(0), scale=1.0 / D).then_inc(rms_sqrt, 1)
            act.wait_ge(bias_mm, 1)
            act.wait_ge(consts_made, 2)
            act.activation(bias_v[:, 0:256], bank(5)[0:HEADS, 0:256], ACT.Copy).then_inc(bias_copied, 1)
            for u in range(UNSPLIT, 10):
                hi(u)
            act.wait_ge(unit_used, 8)
            act.wait_ge(col_ready, 1)
            for b in range(TB):
                act.activation(v_n[:, b, :], bank(4 + b), ACT.Copy, scale=stat(2 + b)).then_inc(v_out, 1)

            def g_sigmoid(i):
                act.wait_ge(g_scaled, i + 1)
                g2 = g_t[:, 2 * i:2 * i + 2, :].rearrange("p c t -> p (c t)")
                act.activation(g2, g2, ACT.Sigmoid).then_inc(g_out, 1)

            hi(10)
            for i in range(5):
                g_sigmoid(i)
                hi(11 + i)
            for block, prob in enumerate((prob1, prob0)):
                act.wait_ge(max_ready, block + 1)
                for h in range(HEADS):
                    act.activation(prob[:, h, :], prob[:, h, :], ACT.Exp, bias=stat(40 + 8 * block + h),
                                   accum_out=stat(56 + 8 * block + h)).then_inc(exp_done, 1)
            hi(U_O)
            for i in range(2):
                act.wait_ge(pooled_done, i + 1)
                for j in range(2):
                    g = 2 * i + j
                    last = act.activation(pool2_hi[:, g, :], bank(6 + i)[:, j * T:(j + 1) * T], ACT.Copy,
                                          scale=consts[:, C_POOL + g:C_POOL + g + 1])
                last.then_inc(pool_hi_out, 1)
            for i in range(0, 6, 2):
                act.wait_ge(probt_done, i + 1)
                act.activation(prob_t[:, 4 * i:4 * i + 4, :].rearrange("p j q -> p (j q)"), bank(i),
                               ACT.Copy).then_inc(probt_out, 1)
            hi(U_O + 1)
            for i in range(5, 8):
                g_sigmoid(i)
            act.wait_ge(probt_done, 6)
            for i in range(2):
                act.wait_ge(pv_done, i + 1)
                act.activation(attn_hi[:, 2 * i:2 * i + 2, :].rearrange("p c t -> p (c t)"), bank(6 + i),
                               ACT.Copy).then_inc(attn_hi_out, 1)
            for u in range(U_O + 2, U_OUT + 4):
                hi(u)
            for jj in range(4):
                act.wait_ge(merged_full, jj + 1)
                act.activation(merged_hi[:, 2 * jj:2 * jj + 2, :].rearrange("p c t -> p (c t)"),
                               mid[:, jj * BANK:(jj + 1) * BANK], ACT.Copy).then_inc(part_hi, 1)

            def squares(b, cols, at):
                act.activation(xg[:, :, :, :].rearrange("p a c s -> p (a c s)")[:, cols], acc[:, b, cols], ACT.Square,
                               accum_out=stat(at)).then_inc(sq_ready, 1)

            def root(b, of, bias):
                act.activation(stat(10 + b), stat(of), ACT.Sqrt, bias=stat(bias), scale=1.0 / D).then_inc(sqrt_ready, 1)

            def normed(b):
                act.wait_ge(rstd_ready, b + 1)
                act.activation(hfn[:, b, :], acc[:, b, :], ACT.Copy, scale=stat(12 + b)).then_inc(norm_ready, 1)

            def logits_evac(b):
                act.wait_ge(logits_mm, b + 1)
                act.activation(lt_sb[:, b, :], bank(b)[:, 0:P], ACT.Copy).then_inc(logits_out, 1)

            for n in range(2):
                for b in range(TB):
                    act.wait_ge(x1_ready, 2 * n + b + 1)
                    if n + b:
                        act.wait_ge(sq_ready, 2 * n + b)
                    squares(b, slice(n * BANK, (n + 1) * BANK), 8 + b if n else (1, 4)[b])
                    if n:
                        act.wait_ge(sq_ready, 3 + b)
                        act.wait_ge(half_mean, b + 1)
                        root(b, 8 + b, 6 + b)
                        logits_evac(b)
            act.wait_ge(wout_done, 4)
            normed(0)
            normed(1)
            for b in range(TB):
                act.wait_ge(top_ready, b + 1)
                last = act.activation(stat(72 + 4 * b, 4), stat(80 + 8 * b, 4), ACT.Exp, bias=stat(20 + b),
                                      accum_out=stat(22 + b))
                last.then_inc(gexp_ready, 1)
            def sigmoid_glu(n):
                act.wait_ge(glu_ready, n + 1)
                act.activation(sg, g_act, ACT.Sigmoid, scale=ALPHA).then_inc(sig_ready, 1)

            def evac_gu(n):
                act.wait_ge(gu_used, n * KD + KD)
                wait_pos(act, gut_done, n)
                act.activation(gu_sb[:, :], bank(0, 2), ACT.Copy).then_inc(gu_out, 1)

            def evac_sel(n):
                act.wait_ge(selt_done, n + 1)
                act.wait_ge(scat_done, 2 * n + 2)
                act.activation(sel[:, :], bank(4)[:, 0:T], ACT.Copy).then_inc(sel_ready, 1)

            def evac_y(n):
                act.wait_ge(dn_used, n * 4 + 4)
                wait_pos(act, scat_done, 2 * n + 2)
                act.activation(y_sb[:, :], bank(7), ACT.Copy).then_inc(y_ready, 1)

            def evac_gathered(n):
                act.wait_ge(gath_done, n + 1)
                wait_pos(act, xt_done, n)
                act.activation(spare[:, :], bank(6), ACT.Copy).then_inc(xn_ready, 1)

            def act_step(e):
                sigmoid_glu(e - 1)
                evac_gu(e)
                evac_gathered(e + 1)
                evac_sel(e - 1)
                evac_y(e - 1)

            act.wait_ge(gates_ready, 1)
            evac_gathered(0)
            act.wait_ge(gates_turned, 1)
            act.activation(gate_rows, bank(5)[0:E, 0:T], ACT.Copy).then_inc(gate_rows_ready, 1)
            evac_gu(0)
            act.wait_ge(lists_ready, 1)
            evac_gathered(1)
            act_step(1)
            with act.Fori(2, E - 1) as e:
                act_step(e)
            sigmoid_glu(E - 2)
            evac_gu(E - 1)
            evac_sel(E - 2)
            evac_y(E - 2)
            sigmoid_glu(E - 1)
            for i in range(4):
                act.wait_ge(pproj_done, i + 1)
                act.activation(pproj[:, i // 2, i % 2 * BANK:(i % 2 + 1) * BANK], bank(i), ACT.Copy).then_inc(pproj_out, 1)
            evac_sel(E - 1)
            evac_y(E - 1)

            act.wait_ge(lists_ready, 1)
            n_extra = act.value_load(lists[0:1, 2 * N_EXTRA:2 * N_EXTRA + 1], min_val=0, max_val=N_EXTRA)
            with act.If(n_extra > 0):
                with act.Fori(0, n_extra) as i:
                    n = i + E
                    evac_gathered(n)
                    evac_sel(n)
                    evac_gu(n)
                    sigmoid_glu(n)
                    evac_y(n)

            for b in range(TB):
                act.wait_ge(x2_ready, b + 1)
                act.wait_ge(sq_ready, 4 + b)
                squares(b, slice(0, D), 8 + b)
            for b in range(TB):
                act.wait_ge(sq_ready, 5 + b)
                root(b, 8 + b, 0)
            for b in range(TB):
                act.wait_ge(rstd_ready, 3 + b)
                for n in range(2):
                    act.wait_ge(gate_done, 2 * b + n + 1)
                    act.activation(gate_s[:, b, n * BANK:(n + 1) * BANK], bank(2 * b + n), ACT.Sigmoid,
                                   scale=stat(12 + b)).then_inc(gate_out, 1)
                act.activation(stat(60 + b), stat(0), ACT.Sqrt)
                for n in range(2):
                    act.wait_ge(x3_ready, 2 * b + n + 1)
                    act.activation(hfn[:, b, n * BANK:(n + 1) * BANK], acc[:, b, n * BANK:(n + 1) * BANK], ACT.Square,
                                   accum_out=stat(16 + 2 * b + n)).then_inc(fin_sq, 1)
                act.wait_ge(fin_sum, b + 1)
                act.activation(stat(72 + b), stat(74 + b), ACT.Sqrt, bias=stat(0), scale=1.0 / D).then_inc(fin_sqrt, 1)
                if b == 0:
                    act.activation(stat(62), stat(0), ACT.Sigmoid)
                act.wait_ge(fin_rstd, b + 1)
                act.activation(gate_s[:, b, BANK:D], gate_s[:, b, BANK:D], ACT.Copy,
                               scale=stat(76 + b)).then_inc(fin_ready, 1)

        @block.tensor
        def _(pe):
            def mm(o, l, r, start, stop, **kw):
                return pe.matmul(o, l, r, start=start, stop=stop, **kw)

            pe.wait_ge(consts_made, 2)
            def three(o, w_hi, w_lo, x_hi, x_lo, start, stop, act_first=False):
                for i, (w, x) in enumerate(((w_hi, x_hi), (w_hi, x_lo), (w_lo, x_hi))):
                    l, r = (x, w) if act_first else (w, x)
                    last = mm(o, l, r, start and i == 0, stop and i == 2)
                return last

            for k in range(KD):
                if k % 4 == 0:
                    pe.wait_ge(s_xt[k // 4], 16)
                    pe.wait_ge(s_win[0] if k else s_first, 16)
                pe.wait_ge(h_ready[k % 2], k // 2 + 1)
                for j in range(2):
                    last = mm(ps[:, j * T:(j + 1) * T], ring[:, 0, k * BLOCK + j * P:k * BLOCK + (j + 1) * P],
                              h_t[:, k, :], k == 0 and j == 0, k == KD - 1, skip_group_check=True)
            last.then_inc(unit_used, 1)
            pe.wait_ge(squares_added, 1)
            mm(bank(4)[:, 0:T], ones[:, :], x_ss, True, True).then_inc(sumsq_done, 1)
            pe.wait_ge(s_relb, 32)
            mm(bank(5)[0:HEADS, 0:T], relb[:, :], onehot, True, True).then_inc(bias_mm, 1)
            landed(pe, 1)
            for j in range(2):
                for k in range(KD):
                    last = mm(bank(1)[:, j * T:(j + 1) * T], ring[:, 1, k * BLOCK + j * P:k * BLOCK + (j + 1) * P],
                              h_t[:, k, :], k == 0, k == KD - 1)
            last.then_inc(unit_used, 1)
            pe.wait_ge(row_ready, 1)
            pe.wait_ge(bias_copied, 1)
            for b in range(TB):
                last = pe.transpose(bank(5)[:, b * P:(b + 1) * P], row256[:, b * P:(b + 1) * P], ident[:, :])
            last.then_inc(row_turned, 1)

            def columns_unit(u, b):
                wait_lo(pe, u)
                for j in range(2):
                    for k in range(KD):
                        at = slice(k * BLOCK + j * P, k * BLOCK + (j + 1) * P)
                        last = three(bank(b)[:, j * T:(j + 1) * T], hi_of(u)[:, at], lo_of(u)[:, at],
                                     h_hi[:, k, :], h_lo[:, k, :], k == 0, k == KD - 1)
                return last.then_inc(unit_used, 1)

            pe.wait_ge(h_lo_ready, 1)
            for u, b in ((2, 2), (3, 3), (4, 6), (5, 7)):
                columns_unit(u, b)
            pe.wait_ge(col_ready, 1)
            for u in (6, 7):
                wait_lo(pe, u)
                for b in range(TB):
                    for k in range(KD):
                        at, t = slice(k * BLOCK, (k + 1) * BLOCK), slice(b * P, (b + 1) * P)
                        last = three(bank(4 + b)[:, (u - 6) * BLOCK:(u - 5) * BLOCK], hi_of(u)[:, at], lo_of(u)[:, at],
                                     h_hi[:, k, t], h_lo[:, k, t], k == 0, k == KD - 1, True)
                last.then_inc(unit_used, 1)

            def g_pair(i):
                if i >= 2:
                    pe.wait_ge(g_scaled, i - 1)
                columns_unit(8 + i, 6 + i % 2)

            pe.wait_ge(u_out, 2)
            g_pair(0)
            g_pair(1)
            pe.wait_ge(qk_out, 4)
            for c in range(4):
                for h in range(2):
                    hp, r = 4 * h + c, slice(h * DH, (h + 1) * DH)
                    last = mm(ps[:, hp * T:(hp + 1) * T], q_t[r, c, P:T], k_t[r, c, :], True, True)
            last.then_inc(scores_done, 1)
            pe.wait_ge(v_out, 2)
            for c in range(4):
                for h in range(2):
                    hp, r = 4 * h + c, slice(h * DH, (h + 1) * DH)
                    last = mm(ps[:, 4 * BANK + hp * P:4 * BANK + (hp + 1) * P], q_t[r, c, 0:P], k_t[r, c, 0:P],
                              True, True)
            last.then_inc(scores_done, 1)
            for i in range(2, 8):
                g_pair(i)
            pe.wait_ge(pooled_ready, 1)
            pe.wait_ge(s_pw, 16)
            for i in (8, 9):
                pe.wait_ge(g_scaled, i - 1)
                for j in range(2):
                    g = 2 * (i - 8) + j
                    last = mm(bank(6 + i % 2)[:, j * T:(j + 1) * T], pw_sb[:, g, :], pooled[:, g, :], True, True)
                last.then_inc(pooled_done, 1)
            pe.wait_ge(prob_ready, 2)
            for j in range(24):
                hp, s = divmod(j, 3)
                src = prob0[:, hp, :] if s == 2 else prob1[:, hp, s * P:(s + 1) * P]
                last = pe.transpose(ps[:, j * P:(j + 1) * P], src, ident[:, :])
                if j % 4 == 3:
                    last.then_inc(probt_done, 1)
            pe.wait_ge(pool_lo_out, 2)
            pe.wait_ge(probt_out, 6)
            for c in range(4):
                for b, kc in ((0, 0), (1, 0), (1, 1)):
                    for h in range(2):
                        hp = 4 * h + c
                        j = 3 * hp + (2 if b == 0 else kc)
                        last = mm(bank(6, 2)[h * DH:(h + 1) * DH, c * T + b * P:c * T + (b + 1) * P],
                                  v_n[:, kc, (2 * c + h) * DH:(2 * c + h + 1) * DH], prob_t[:, j, :],
                                  kc == 0, kc == b)
                if c % 2:
                    last.then_inc(pv_done, 1)
            for which, hi_in, lo_in, first, done in ((0, pool2_hi, pool2_lo, 0, po_done),
                                                     (1, attn_hi, attn_lo, 4, ao_done)):
                pe.wait_ge(attn_out if which else pool_lo_out, 2)
                wait_lo(pe, U_O + 2 * which)
                wait_lo(pe, U_O + 2 * which + 1)
                for jj in range(4):
                    for j in range(2):
                        col = (2 * jj + j) * P
                        for k in range(4):
                            u, at = U_O + 2 * which + k // 2, slice(k % 2 * D + col, k % 2 * D + col + P)
                            last = three(bank(first + jj)[:, j * T:(j + 1) * T], hi_of(u)[:, at], lo_of(u)[:, at],
                                         hi_in[:, k, :], lo_in[:, k, :], k == 0, k == 3)
                    last.then_inc(done, 1)
            rw = consts[:, C_RW:C_RW + KD * E].rearrange("p (c e) -> p c e", c=KD)

            def turn_x(b, chunks):
                for c in chunks:
                    last = pe.transpose(bank(4 + 2 * b, 2)[:, c * P:(c + 1) * P], acc[:, b, c * P:(c + 1) * P],
                                        ident[:, :])
                last.then_inc(turned, 1)

            def w_out_part(b, n, chunks):
                for k in chunks:
                    u, at = U_OUT + 2 * n + k // 4, slice(k % 4 * BANK, (k % 4 + 1) * BANK)
                    if k % 4 == 0:
                        wait_lo(pe, u)
                    if b == 0 and n == 0:
                        pe.wait_ge(merged_ready, k // 2 + 1)
                    last = three(bank(2 * b + n), hi_of(u)[:, at], lo_of(u)[:, at], merged_hi[:, k, b * P:(b + 1) * P],
                                 merged_lo[:, k, b * P:(b + 1) * P], k == 0, k == KD - 1, True)
                if k == KD - 1:
                    last.then_inc(wout_done, 1)

            def logits_t(b, chunks):
                for c in chunks:
                    q = c % 4
                    last = mm(bank(b)[E * q:E * (q + 1), 0:P], rw[:, c, :], hf_t[b][:, c, :], c < 4, c >= 4)
                if c == KD - 1:
                    last.then_inc(logits_mm, 1)

            def logits(b):
                pe.wait_ge(logits_out, b + 1)
                pe.transpose(bank(b)[:, P:2 * P], lt_sb[:, b, :], ident[:, :]).then_inc(logits_done, 1)

            w_out_part(0, 0, range(KD))
            w_out_part(1, 0, range(KD))
            w_out_part(0, 1, range(0, 4))
            pe.wait_ge(merged_ready, 4)
            for b in range(TB):
                pe.wait_ge(x1_ready, b + 1)
                turn_x(b, range(0, 4))
            w_out_part(0, 1, range(4, KD))
            w_out_part(1, 1, range(0, 1))
            pe.wait_ge(x1_ready, 3)
            turn_x(0, range(4, KD))
            w_out_part(1, 1, range(1, 3))
            pe.wait_ge(s_pack, 16)
            pe.wait_ge(turned_out, 3)
            logits_t(0, range(KD))
            w_out_part(1, 1, range(3, 4))
            logits(0)
            w_out_part(1, 1, range(4, KD))
            pe.wait_ge(chosen_ready, 1)
            mm(bank(2)[:, 0:E], tri[:, :], chosen[:, 0, :], True, True)
            mm(bank(2)[:, E:2 * E], ones[:, :], chosen[:, 0, :], True, False)
            pe.wait_ge(x1_ready, 4)
            turn_x(1, range(4, KD))
            pe.wait_ge(turned_out, 4)
            logits_t(1, range(KD))
            logits(1)
            pe.wait_ge(chosen_ready, 2)
            mm(bank(2)[:, E:2 * E], tri[:, :], chosen[:, 1, :], False, True).then_inc(rank_done, 1)

            def gather(n, h, scattered):
                pe.wait_ge(pick_ready, n + 1)
                wait_pos(pe, added, 2 * scattered)
                wait_pos(pe, xg_ready, n)
                for b in range(TB):
                    for half in range(2):
                        last = mm(bank(6)[SLOTS * half:SLOTS * (half + 1), :], pick[:, h, b, :],
                                  hfn[:, b, half * BANK:(half + 1) * BANK], b == 0, b == TB - 1)
                last.then_inc(gath_done, 1)

            def turn_gathered(n):
                pe.wait_ge(xn_ready, n + 1)
                for c in range(4):
                    last = pe.transpose(bank(6)[:, c * P:(c + 1) * P], spare[:, c * P:(c + 1) * P], ident[:, :])
                last.then_inc(xt_done, 1)

            def turn_sel(n, scattered):
                pe.wait_ge(pickg_ready, n + 1)
                pe.wait_ge(added, 2 * scattered)
                for b in range(TB):
                    last = pe.transpose(bank(4)[:, b * P:(b + 1) * P],
                                        pick_g[:, b, :, :].rearrange("p a s -> p (a s)"), ident[:, :])
                last.then_inc(selt_done, 1)

            def gate_up(n, h, landed):
                pe.wait_ge(xg_ready, n + 1)
                wait_pos(pe, gu_out, n)
                for k in range(KD):
                    pe.wait_ge(s_gu[h][k], landed)
                    for q in range(4):
                        half = slice(SLOTS * (q % 2), SLOTS * (q % 2 + 1))
                        last = mm(bank(q // 2)[half, :], xg[:, h, k, :], ring[:, 8 * h + k, q * BANK:(q + 1) * BANK],
                                  k == 0, k == KD - 1)
                    last.then_inc(gu_used, 1)

            def down(n, scattered, landed, first=16, arrivals=s_dn):
                pe.wait_ge(hid_ready, n + 1)
                wait_pos(pe, added, 2 * scattered)
                hid4 = hid.rearrange("p (b q a s) -> p b q a s", b=2, q=2, a=2)
                for u in range(4):
                    pe.wait_ge(arrivals[u], landed)
                    for j in range(2):
                        k = 2 * u + j
                        for half in range(2):
                            last = mm(bank(7)[SLOTS * half:SLOTS * (half + 1), :], hid4[:, k // 4, k % 2, k // 2 % 2, :],
                                      slot2(first + u)[:, j, half * BANK:(half + 1) * BANK], k == 0, k == KD - 1)
                    last.then_inc(dn_used, 1)

            def turn_gu(n):
                pe.wait_ge(gu_out, n + 1)
                wait_pos(pe, gut_read, n)
                pairs = gu_sb[:, :].rearrange("p (t r k) -> p t r k", t=4, k=2)
                for kind in range(2):
                    for t in range(4):
                        last = pe.transpose(bank(2 + kind)[:, t * P:(t + 1) * P], pairs[:, t, :, kind], ident[:, :])
                last.then_inc(gut_done, 1)

            def scatter(n, scattered, gathered):
                pe.wait_ge(y_ready, n + 1)
                pe.wait_ge(sel_ready, n + 1)
                pe.wait_ge(added, 2 * scattered)
                for b in range(TB):
                    if b == 1:
                        pe.wait_ge(xg_ready, gathered)
                    for half in range(2):
                        r = slice(SLOTS * half, SLOTS * (half + 1))
                        last = mm(bank(4 + 2 * b + half), sel[r, b * P:(b + 1) * P], y_sb[r, :], True, True)
                    last.then_inc(scat_done, 1)

            pe.wait_ge(norm_ready, 2)
            gather(0, 0, 0)
            mm(bank(3)[0:1, 0:E], ones[:, 0:1], chosen[:, 0, :], True, False)
            mm(bank(3)[0:1, 0:E], ones[:, 0:1], chosen[:, 1, :], False, True).then_inc(count_done, 1)
            pe.wait_ge(gates_ready, 1)
            for b in range(TB):
                last = pe.transpose(bank(5)[0:E, b * P:(b + 1) * P], gates[:, b, :], ident[:, :])
            last.then_inc(gates_turned, 1)
            turn_gathered(0)
            gate_up(0, 0, 16)
            gather(1, 1, 0)
            pe.wait_ge(counts_read, 1)
            turn_gu(0)
            turn_gathered(1)
            pe.wait_ge(gate_rows_ready, 1)
            pe.wait_ge(s_bd, 32)
            pe.wait_ge(xg_ready, 2)
            for b in range(TB):
                for half in range(2):
                    last = mm(bank(4 + 2 * b + half), gate_rows[:, b * P:(b + 1) * P], bd_half[half], True, True)
                last.then_inc(scat_done, 1)

            def pe_step(e, h, gu_landed):
                gate_up(e, h, gu_landed)
                gather(e + 1, 1 - h, e)
                turn_sel(e - 1, e)
                down(e - 1, e, e * 16)
                turn_gathered(e + 1)
                turn_gu(e)
                scatter(e - 1, e, e + 2)

            pe_step(1, 1, 16)
            with pe.Fori(1, E // 2 - 1) as it:
                for h in range(2):
                    pe_step(2 * it + h, h, it * 16 + 16)
            pe_step(E - 2, 0, 8 * E)
            gate_up(E - 1, 1, 8 * E)
            turn_sel(E - 2, E - 1)
            down(E - 2, E - 1, 16 * (E - 1))
            turn_gu(E - 1)
            scatter(E - 2, E - 1, E)
            pe.wait_ge(s_ple_proj, 32)
            pe.wait_ge(gu_out, E)
            for i in range(4):
                b, n = divmod(i, 2)
                if i == 2:
                    pe.wait_ge(gut_read, E)
                for k in range(2):
                    last = mm(bank(i), pt_sb[:, k, b * P:(b + 1) * P], wpp[:, k, n * BANK:(n + 1) * BANK],
                              k == 0, k == 1)
                last.then_inc(pproj_done, 1)
            turn_sel(E - 1, E)
            down(E - 1, E, 16, 0, s_dn_last)
            scatter(E - 1, E, E)

            pe.wait_ge(lists_ready, 1)
            n_extra = pe.value_load(lists[0:1, 2 * N_EXTRA:2 * N_EXTRA + 1], min_val=0, max_val=N_EXTRA)
            with pe.If(n_extra > 0):
                with pe.Fori(0, n_extra) as i:
                    n = i + E
                    gather(n, 1, n + 1)
                    turn_sel(n, n + 1)
                    turn_gathered(n)
                    pe.wait_ge(pproj_out, 4)
                    gate_up(n, 1, i * 16 + (E // 2 + 1) * 16)
                    turn_gu(n)
                    down(n, n + 1, i * 16 + 32, 0, s_dn_last)
                    scatter(n, n + 1, n + 1)

            pe.wait_ge(x2_ready, 1)
            turn_x(0, range(KD))
            for b in range(TB):
                pe.wait_ge(turned_out, 5 + b)
                for n in range(2):
                    pe.wait_ge(pproj_out, 2 * b + n + 1)
                    for k in range(KD):
                        pe.wait_ge(s_dn[k // 2], 16 * E)
                        last = mm(bank(2 * b + n), hp_t[:, k, b, :], wpg[:, k, n * BANK:(n + 1) * BANK],
                                  k == 0, k == KD - 1)
                    last.then_inc(gate_done, 1)
                    if b == 0 and n == 0:
                        pe.wait_ge(x2_ready, 2)
                        turn_x(1, range(KD))

        @block.vector
        def _(dve):
            chain = Chain(dve, dve_chain)
            tt, ts, stt = dve.tensor_tensor, dve.tensor_scalar, dve.scalar_tensor_tensor
            dve.memset(stat(0), EPS).then_inc(eps_ready, 1)
            dve.wait_ge(s_norms, 16)
            for c in range(1, KD, 2):
                dve.wait_ge(s_xt[c // 4], 16)
                ts(h_t[:, c, :], x_raw[:, c, :], consts[:, C_MIX + c:C_MIX + c + 1], None,
                   ALU.mult).then_inc(h_ready[1], 1)
            for c in range(1, KD, 2):
                tt(x_sq[:, c, :], x_raw[:, c, :], x_raw[:, c, :], ALU.mult).then_inc(squared, 1)
            dve.wait_ge(squared, KD)
            dve.tensor_reduce(x_ss, x_sq.rearrange("p c t -> p t c"), AX, ALU.add).then_inc(squares_added, 1)
            dve.wait_ge(h_hi_ready, 1)
            tt(h_lo, h_t, h_hi.bitcast(F32), ALU.subtract).then_inc(h_lo_ready, 1)

            def lo(u):
                dve.wait_ge(hi_ready, split_in(u))
                tt(lo_of(u), ring[:, PLACES[u][0], :], hi_of(u).bitcast(F32), ALU.subtract).then_inc(lo_ready, 1)

            dve.wait_ge(rms_sqrt, 1)
            dve.reciprocal(row256[:, :], row256[:, :]).then_inc(row_ready, 1)
            lo(2)
            dve.wait_ge(cnt_ready, 1)
            for g, w in enumerate(WINDOWS):
                last = dve.reciprocal(inv_cnt[:, g, 0:w], inv_cnt[:, g, 0:w])
            last.then_inc(inv_ready, 1)
            dve.wait_ge(row_turned, 1)
            dve.tensor_copy(stat(2, 2), bank(5)[:, 0:T:P]).then_inc(col_ready, 1)
            rstd2 = row256[:, :].unsqueeze(1).to_broadcast([P, 2, T])

            def times_rstd(out, b):
                return tt(out, bank(b).rearrange("p (c t) -> p c t", c=2), rstd2, ALU.mult)

            dve.wait_ge(row_ready, 1)
            for j in range(2):
                dve.wait_ge(unit_used, 1 + j)
                times_rstd(q_t[:, 2 * j:2 * j + 2, :], j).then_inc(qk_out, 1)
                lo(3 + j)
            for j in range(2):
                dve.wait_ge(unit_used, 3 + j)
                times_rstd(k_t[:, 2 * j:2 * j + 2, :], 2 + j).then_inc(qk_out, 1)
                lo(5 + j)
            for j in range(2):
                dve.wait_ge(unit_used, 5 + j)
                times_rstd(u_t[:, 2 * j:2 * j + 2, :], 6 + j).then_inc(u_out, 1)
                lo(7 + j)
            lo(9)
            lo(10)

            def scale_g(i):
                dve.wait_ge(unit_used, 9 + i)
                times_rstd(g_t[:, 2 * i:2 * i + 2, :], 6 + i % 2).then_inc(g_scaled, 1)

            def masked_scores(i, prob, src, bs):
                dve.wait_ge(s_bias_in, 32)
                dve.wait_ge(scores_done, i + 1)
                chain(stt(out=prob, in0=src.rearrange("p (h k) -> p h k", h=HEADS), scalar=DH ** -0.5, in1=bs,
                          op0=ALU.mult, op1=ALU.add))

            def maxima(i, prob):
                chain(dve.tensor_reduce(stat(24 + 8 * i, 8), prob, AX, ALU.max))
                ts(stat(40 + 8 * i, 8), stat(24 + 8 * i, 8), -1.0, None, ALU.mult).then_inc(max_ready, 1)

            def over_sums(i, prob):
                dve.wait_ge(exp_done, 8 + 8 * i)
                chain(dve.reciprocal(stat(24 + 8 * i, 8), stat(56 + 8 * i, 8)))
                tt(prob, prob, stat(24 + 8 * i, 8).unsqueeze(2).to_broadcast([P, HEADS, prob.shape[2]]),
                   ALU.mult).then_inc(prob_ready, 1)

            for i in range(8):
                scale_g(i)
                if i < 5:
                    lo(11 + i)
                if i == 2:
                    masked_scores(0, prob1, ps[:, 0:4 * BANK], bias)
                if i == 3:
                    maxima(0, prob1)
                if i == 5:
                    masked_scores(1, prob0, ps[:, 4 * BANK:6 * BANK], bias[:, :, P:T])
                    maxima(1, prob0)
                if i == 6:
                    over_sums(0, prob1)
                if i == 7:
                    over_sums(1, prob0)
            for i in range(2):
                dve.wait_ge(pool_hi_out, i + 1)
                for j in range(2):
                    g = 2 * i + j
                    last = stt(out=pool2_lo[:, g, :], in0=bank(6 + i)[:, j * T:(j + 1) * T],
                               scalar=consts[:, C_POOL + g:C_POOL + g + 1], in1=pool2_hi[:, g, :].bitcast(F32),
                               op0=ALU.mult, op1=ALU.subtract)
                last.then_inc(pool_lo_out, 1)
            for i in range(1, 6, 2):
                dve.wait_ge(probt_done, i + 1)
                dve.tensor_copy(prob_t[:, 4 * i:4 * i + 4, :].rearrange("p j q -> p (j q)"),
                                bank(i)).then_inc(probt_out, 1)
            lo(U_O + 1)
            for i in range(2):
                dve.wait_ge(attn_hi_out, i + 1)
                tt(attn_lo[:, 2 * i:2 * i + 2, :].rearrange("p c t -> p (c t)"), bank(6 + i),
                   attn_hi[:, 2 * i:2 * i + 2, :].rearrange("p c t -> p (c t)").bitcast(F32),
                   ALU.subtract).then_inc(attn_out, 1)
            dve.wait_ge(g_out, 8)
            for jj in range(4):
                dve.wait_ge(po_done, jj + 1)
                m = mid[:, jj * BANK:(jj + 1) * BANK]
                chain(tt(m, bank(jj), g_t[:, 8 + 2 * jj:10 + 2 * jj, :].rearrange("p c t -> p (c t)"), ALU.mult))
                if jj == 0:
                    lo(U_OUT)
            lo(U_OUT + 1)
            for jj in range(4):
                dve.wait_ge(ao_done, jj + 1)
                m = mid[:, jj * BANK:(jj + 1) * BANK]
                chain(tt(branch, bank(4 + jj), g_t[:, 2 * jj:2 * jj + 2, :].rearrange("p c t -> p (c t)"),
                         ALU.mult))
                tt(m, m, branch, ALU.add).then_inc(merged_full, 1)
                dve.wait_ge(merged_full, jj + 1)
                dve.wait_ge(part_hi, jj + 1)
                tt(merged_lo[:, 2 * jj:2 * jj + 2, :].rearrange("p c t -> p (c t)"), m,
                   merged_hi[:, 2 * jj:2 * jj + 2, :].rearrange("p c t -> p (c t)").bitcast(F32),
                   ALU.subtract).then_inc(merged_ready, 1)
            dve.wait_ge(s_x, 16)

            def turned_evac(n, b, col, view, first=0, chunks=KD):
                dve.wait_ge(turned, n + 1)
                tt(view[:, first:first + chunks, :],
                   bank(4 + 2 * b, 2).rearrange("p (c t) -> p c t", c=KD)[:, first:first + chunks, :],
                   consts[:, col + first:col + first + chunks].unsqueeze(2).to_broadcast([P, chunks, P]),
                   ALU.mult).then_inc(turned_out, 1)

            def make_rstd(n, b):
                dve.wait_ge(sqrt_ready, n + 1)
                dve.reciprocal(stat(12 + b), stat(10 + b)).then_inc(rstd_ready, 1)
                dve.wait_ge(rstd_ready, n + 1)

            idx = hot_g[:, 0, 0:16].bitcast(U32)
            idx1 = hot_g[:, 1, 0:8]
            logits = rank1

            def choose(b):
                dve.wait_ge(logits_done, b + 1)
                chain(dve.tensor_reduce(logits[:, b, :], bank(b)[:, P:2 * P].rearrange("p (q e) -> p e q", q=4), AX,
                                        ALU.add))
                chain(stt(out=logits[:, b, :], in0=logits[:, b, :], scalar=stat(12 + b), in1=rb_bc[:, :],
                          op0=ALU.mult, op1=ALU.add))
                chain(dve.max(stat(80 + 8 * b, 8), logits[:, b, :]))
                chain(dve.max_index(idx[:, 8 * b:8 * b + 8], stat(80 + 8 * b, 8), logits[:, b, :]))
                chain(ts(idx1[:, 4 * b:4 * b + 4], idx[:, 8 * b:8 * b + 4], 1.0, None, ALU.add))
                chain(tt(hot[:, 4 * b:4 * b + 4, :], iota1[:, 0:E].unsqueeze(1).to_broadcast([P, TOP_K, E]),
                         idx1[:, 4 * b:4 * b + 4].unsqueeze(2).to_broadcast([P, TOP_K, E]), ALU.is_equal))
                dve.tensor_reduce(chosen[:, b, :], hot[:, TOP_K * b:TOP_K * (b + 1), :]
                                  .rearrange("p k e -> p e k"), AX, ALU.add).then_inc(chosen_ready, 1)
                ts(stat(20 + b), stat(80 + 8 * b), -1.0, None, ALU.mult).then_inc(top_ready, 1)

            def add_piece(b, n):
                cols = slice(n * BANK, (n + 1) * BANK)
                dve.wait_ge(wout_done, 2 * n + b + 1)
                tt(acc[:, b, cols], acc[:, b, cols], bank(2 * b + n), ALU.add).then_inc(x1_ready, 1)

            add_piece(0, 0)
            add_piece(1, 0)
            dve.wait_ge(s_pack, 16)
            dve.wait_ge(s_rb, 16)
            for b in range(TB):
                turned_evac(b, b, C_FFN, hf_t[b], 0, 4)
            for b in range(TB):
                dve.wait_ge(sq_ready, b + 1)
                ts(stat(6 + b), stat((1, 4)[b]), 1.0 / D, EPS, ALU.mult, ALU.add).then_inc(half_mean, 1)
            for b in range(TB):
                add_piece(b, 1)
                turned_evac(2 + b, b, C_FFN, hf_t[b], 4, 4)
                make_rstd(b, b)
                choose(b)
            dve.wait_ge(chosen_ready, 2)
            dve.wait_ge(rank_done, 1)
            chain(stt(out=rank1[:, :, :], in0=bank(2)[:, 0:TB * E].rearrange("p (b e) -> p b e", b=TB), scalar=1.0,
                      in1=chosen[:, :, :], op0=ALU.add, op1=ALU.mult))

            def column(table, e):
                one = table[:, :, e:e + 1] if isinstance(e, int) else table[:, :, bass.ds(e, 1)]
                return one.to_broadcast([P, TB, SLOTS])

            def make_pick(n, h, e, gathered, first=0):
                wait_pos(dve, gath_done, gathered)
                slots = iota1[:, 0:SLOTS] if isinstance(first, int) else iota1[:, bass.ds(first, SLOTS)]
                tt(pick[:, h, :, :], slots.unsqueeze(1).to_broadcast([P, TB, SLOTS]), column(rank1, e),
                   ALU.is_equal).then_inc(pick_ready, 1)

            def make_pick_g(n, h, e):
                wait_pos(dve, selt_done, n)
                dve.wait_ge(pick_ready, n + 1)
                for a in range(2):
                    ins = tt(pick_g[:, :, a, :], pick[:, h, :, :], column(gates, e), ALU.mult)
                ins.then_inc(pickg_ready, 1)

            def xg_evac(n, h, served):
                dve.wait_ge(xt_done, n + 1)
                wait_pos(dve, gu_used, served * KD)
                tt(xg[:, h, :, :].rearrange("p (a c) s -> p a c s", a=2),
                   bank(6).rearrange("p (c a s) -> p a c s", c=4, a=2),
                   consts[:, C_FFN:C_FFN + KD].rearrange("p (a c) -> p a c", a=2).unsqueeze(3)
                   .to_broadcast([P, 2, 4, SLOTS]), ALU.mult).then_inc(xg_ready, 1)

            bgu = consts[:, C_BGU:C_BGU + 16 * E].rearrange("p (e k t) -> p e k t", e=E, k=2)

            def expert_bias(e, kind):
                one = bgu[:, e, kind, :] if isinstance(e, int) else \
                    bgu[:, bass.ds(e, 1), kind, :].rearrange("p o t -> p (o t)")
                return one.unsqueeze(2).to_broadcast([P, 8, SLOTS])

            def swiglu(n, e):
                def tiles(x):
                    return x.rearrange("p (t s) -> p t s", s=SLOTS)
                dve.wait_ge(gut_done, n + 1)
                chain(tt(tiles(g_act), tiles(bank(2)), expert_bias(e, 0), ALU.add))
                ts(g_act, g_act, LIMIT, None, ALU.min).then_inc(glu_ready, 1)
                tt(tiles(l_act), tiles(bank(3)), expert_bias(e, 1), ALU.add).then_inc(gut_read, 1)
                dve.wait_ge(gut_read, n + 1)
                chain(ts(l_act, l_act, LIMIT, -LIMIT, ALU.min, ALU.max))
                dve.wait_ge(glu_ready, n + 1)
                chain(stt(out=l_act, in0=l_act, scalar=1.0, in1=g_act, op0=ALU.add, op1=ALU.mult))
                dve.wait_ge(sig_ready, n + 1)
                wait_pos(dve, dn_used, n * 4)
                dve.wait_ge(scat_done, 2)
                tt(hid, l_act, sg, ALU.mult).then_inc(hid_ready, 1)

            def add_back(j):
                for b in range(TB):
                    dve.wait_ge(scat_done, 2 * j + b + 1)
                    tt(acc[:, b, :], acc[:, b, :], bank(4 + 2 * b, 2), ALU.add).then_inc(added, 1)

            make_pick(0, 0, 0, 0)
            dve.wait_ge(gexp_ready, 2)
            chain(dve.reciprocal(stat(22, 2), stat(22, 2)))
            chain(tt(stat(72, 8).rearrange("p (b k) -> p b k", b=TB), stat(72, 8).rearrange("p (b k) -> p b k", b=TB),
                     stat(22, 2).unsqueeze(2).to_broadcast([P, TB, TOP_K]), ALU.mult))
            chain(tt(hot_g[:, :, :], hot[:, :, :], stat(72, 8).unsqueeze(2).to_broadcast([P, TB * TOP_K, E]), ALU.mult))
            for b in range(TB):
                ins = dve.tensor_reduce(gates[:, b, :], hot_g[:, TOP_K * b:TOP_K * (b + 1), :]
                                        .rearrange("p k e -> p e k"), AX, ALU.add)
            ins.then_inc(gates_ready, 1)
            dve.wait_ge(gates_ready, 1)
            xg_evac(0, 0, 0)
            make_pick_g(0, 0, 0)
            dve.wait_ge(count_done, 1)
            has, place = spare[0:1, 0:3 * E], spare[0:1, 3 * E:6 * E]
            picked = spare[0:1, 6 * E:9 * E].rearrange("p (b e) -> p b e", b=3)
            place3 = place.rearrange("p (b e) -> p b e", b=3)
            sums = small[0:1, 24:24 + 2 * N_EXTRA + 1]
            for b in range(3):
                ins = ts(has[:, b * E:(b + 1) * E], bank(3)[0:1, 0:E], float(SLOTS * (b + 1)), None, ALU.is_gt)
            ins.then_inc(counts_read, 1)
            dve.wait_ge(counts_read, 1)
            chain(dve.tensor_tensor_scan(place, ones[0:1, 0:3 * E], has, 0.0, ALU.mult, ALU.add))
            chain(tt(place, place, has, ALU.mult))
            experts = iota1[0:1, 0:E].unsqueeze(1).to_broadcast([1, 3, E])
            blocks = iota1[0:1, 0:3].unsqueeze(2).to_broadcast([1, 3, E])
            for i in range(N_EXTRA):
                for j, code in enumerate((experts, blocks)):
                    chain(stt(out=picked, in0=place3, scalar=float(i + 1), in1=code, op0=ALU.is_equal,
                              op1=ALU.mult, accum_out=sums[:, j * N_EXTRA + i:j * N_EXTRA + i + 1]))
            chain(dve.tensor_reduce(sums[:, 2 * N_EXTRA:], has, AX, ALU.add))
            chain(ts(sums[:, 0:N_EXTRA], sums[:, 0:N_EXTRA], -1.0, 0.0, ALU.add, ALU.max))
            chain(ts(sums[:, N_EXTRA:2 * N_EXTRA], sums[:, N_EXTRA:2 * N_EXTRA], float(SLOTS), None, ALU.mult))
            dve.tensor_copy(lists[:, :], sums).then_inc(lists_ready, 1)

            make_pick(1, 1, 1, 0)
            xg_evac(1, 1, 0)

            def dve_step(e, h):
                swiglu(e - 1, e - 1)
                add_back(e - 1)
                make_pick(e + 1, 1 - h, e + 1, e)
                xg_evac(e + 1, 1 - h, e)
                make_pick_g(e, h, e)

            dve_step(1, 1)
            steps = 3
            start = chain.n
            with dve.Fori(1, E // 2 - 1) as it:
                for h in range(2):
                    chain.n = (it - 1) * (2 * steps) + (start + h * steps)
                    dve_step(2 * it + h, h)
            chain.n = start + steps * (E - 4)
            dve_step(E - 2, 0)
            swiglu(E - 2, E - 2)
            add_back(E - 2)
            make_pick_g(E - 1, 1, E - 1)
            swiglu(E - 1, E - 1)
            add_back(E - 1)
            add_back(E)
            dve.wait_ge(added, 2 * E + 2)
            start = chain.n

            n_extra = dve.value_load(lists[0:1, 2 * N_EXTRA:2 * N_EXTRA + 1], min_val=0, max_val=N_EXTRA)
            with dve.If(n_extra > 0):
                with dve.Fori(0, n_extra) as i:
                    n = i + E
                    e = dve.value_load(lists[0:1, bass.ds(i, 1)], min_val=0, max_val=E - 1)
                    first = dve.value_load(lists[0:1, bass.ds(i + N_EXTRA, 1)], min_val=0, max_val=T - SLOTS)
                    chain.n = i * steps + start
                    make_pick(n, 1, e, n, first)
                    make_pick_g(n, 1, e)
                    xg_evac(n, 1, n)
                    swiglu(n, e)
                    add_back(n + 1)
                    dve.wait_ge(added, 2 * n + 4)
            chain = Chain(dve, dve_tail_chain)

            for b in range(TB):
                dve.memset(stat(4 + b), 0.0).then_inc(x2_ready, 1)
            for b in range(TB):
                turned_evac(4 + b, b, C_PLE, hp_t[:, :, b, :])
                make_rstd(2 + b, b)
            dve.wait_ge(s_fg, 16)
            for b in range(TB):
                for n in range(2):
                    cols = slice(n * BANK, (n + 1) * BANK)
                    dve.wait_ge(gate_out, 2 * b + n + 1)
                    dve.wait_ge(pproj_out, 2 * b + n + 1)
                    chain(tt(gate_s[:, b, cols], gate_s[:, b, cols], pproj[:, b, cols], ALU.mult))
                    tt(acc[:, b, cols], acc[:, b, cols], gate_s[:, b, cols], ALU.add).then_inc(x3_ready, 1)
                    dve.wait_ge(x3_ready, 2 * b + n + 1)
                    chain(tt(gate_s[:, b, cols], acc[:, b, cols], fg_bc[:, cols], ALU.mult))
                dve.wait_ge(fin_sq, 2 * b + 2)
                tt(stat(74 + b), stat(16 + 2 * b), stat(17 + 2 * b), ALU.add).then_inc(fin_sum, 1)
                dve.wait_ge(fin_sqrt, b + 1)
                dve.reciprocal(stat(76 + b), stat(72 + b)).then_inc(fin_rstd, 1)
                dve.wait_ge(fin_rstd, b + 1)
                ts(gate_s[:, b, 0:BANK], gate_s[:, b, 0:BANK], stat(76 + b), None, ALU.mult).then_inc(fin_ready, 1)


def kernel(**inputs):
    from concourse import bacc
    from concourse.bass_utils import run_bass_kernel_spmd

    def f(name, *shape):
        return np.ascontiguousarray(inputs[name]).reshape(shape)

    columns = [f(n, -1, P).T for n in ("norm_mix_g", "norm_ffn_g", "norm_ple_g", "pool_scale")]
    router = f("router_w", KD, P, E).transpose(1, 0, 2).reshape(P, KD * E)
    bgu = f("b_gate_up", E, 2, 2, 2, P, 2).transpose(4, 0, 5, 1, 3, 2).reshape(P, E * 16)
    dist = T - 1 - np.arange(T)
    exact = BUCKETS // 2
    large = exact + (np.log(np.maximum(dist, 1) / exact) / math.log(MAX_DISTANCE / exact) * exact).astype(int)
    bucket = np.where(dist < exact, dist, np.minimum(large, BUCKETS - 1))
    arrays = {
        "x": f("x", T, D), "x_t": np.ascontiguousarray(f("x", T, D).T),
        "p_t": np.ascontiguousarray(f("p", T, PLE).T),
        "pack": np.ascontiguousarray(np.concatenate(columns + [router, bgu], axis=1)),
        "rel_bias": f("rel_bias", BUCKETS, HEADS),
        "bucket_of": (np.arange(BUCKETS)[:, None] == bucket[None, :]).astype(np.float32),
        "w_in": np.ascontiguousarray(f("w_in", KD, P, N_IN, BLOCK).transpose(2, 1, 0, 3)).reshape(N_IN, P, NW),
        "pool_w": f("pool_w", GROUPS, P, P),
        "w_o_attn": f("w_o_attn", AW, D), "w_o_pool": f("w_o_pool", AW, D), 
        "w_out": np.ascontiguousarray(f("w_out", 2, 4, P, 2, BANK).transpose(3, 0, 2, 1, 4)).reshape(4, P, NW),
        "router_b": f("router_b", E), "w_gate_up": f("w_gate_up", E, D, NW), "w_down": f("w_down", E, D, D),
        "b_down": f("b_down", E, D), "w_ple_gate": f("w_ple_gate", D, D), "w_ple_proj": f("w_ple_proj", PLE, D),
        "norm_final_g": f("norm_final_g", D),
    }
    nc = bacc.Bacc("TRN2", target_bir_lowering=False, num_devices=1)
    args = {n: nc.dram_tensor(f"in_{n}", a.shape, mybir.dt.from_np(a.dtype), kind="ExternalInput").ap()
            for n, a in arrays.items()}
    out = nc.dram_tensor("out_0", (T, D), F32, kind="ExternalOutput").ap()
    block_kernel(nc, **args, out=out)
    r = run_bass_kernel_spmd(nc, [{f"in_{n}": a for n, a in arrays.items()}], core_ids=[0])
    return r.results[0]["out_0"].reshape(1, T, D)
```
